# Optimizing a Trainium2 kernel written in Bass

```python
import math
import jax, jax.numpy as jnp
from jax import lax
import numpy as np
import jax
import jax.numpy as jnp

D_MODEL = 1024
BATCH = 1
SEQ = 512
DEPTH = 2

RMS_EPS = 1e-6
LN_EPS = 1e-5
MIX_WIDTH = D_MODEL
POOL_WIDTH = MIX_WIDTH // 2
POOL_WINDOWS = (2, 4, 8, 16)
POOL_GROUPS = len(POOL_WINDOWS)
POOL_GROUP_DIM = POOL_WIDTH // POOL_GROUPS
SSM_WIDTH = MIX_WIDTH - POOL_WIDTH
SSM_GROUP_DIM = 16
SSM_GROUPS = SSM_WIDTH // SSM_GROUP_DIM
SSM_STATE = 64
DT_MIN = 0.001
DT_MAX = 0.1
CONV_CHANNELS = D_MODEL
CONV_KERNEL = 31
N_EVEN = (DEPTH + 1) // 2
N_ODD = DEPTH // 2


def _rmsnorm(x, g):
    x32 = x.astype(jnp.float32)
    y = x32 * lax.rsqrt(jnp.mean(x32 * x32, axis=-1, keepdims=True) + RMS_EPS)
    return (y * g.astype(jnp.float32)).astype(x.dtype)

def _multiscale_pool(u, pool_w, pool_scale):
    b, s, _ = u.shape
    u32 = u.astype(jnp.float32).reshape(b, s, POOL_GROUPS, POOL_GROUP_DIM)
    csum = jnp.cumsum(u32, axis=1)
    pos = jnp.arange(1, s + 1, dtype=jnp.float32)[None, :, None]
    outs = []
    for g, w in enumerate(POOL_WINDOWS):
        c = csum[:, :, g, :]
        lag = jnp.pad(c, ((0, 0), (w, 0), (0, 0)))[:, :s, :]
        outs.append((c - lag) / jnp.minimum(pos, float(w)) - u32[:, :, g, :])
    pooled = jnp.stack(outs, axis=2)
    mixed = jnp.einsum('bsgc,gcd->bsgd', pooled, pool_w.astype(jnp.float32))
    return (mixed.reshape(b, s, POOL_WIDTH) * pool_scale.astype(jnp.float32)).astype(u.dtype)

def _scan_combine(left, right):
    a1r, a1i, b1r, b1i = left
    a2r, a2i, b2r, b2i = right
    ar = a2r * a1r - a2i * a1i
    ai = a2r * a1i + a2i * a1r
    br = a2r * b1r - a2i * b1i + b2r
    bi = a2r * b1i + a2i * b1r + b2i
    return (ar, ai, br, bi)

def _s5(u, log_dt, a_re, a_im, b_re, b_im, c_re, c_im, d_skip, w_glu):
    bsz, s, _ = u.shape
    f32 = jnp.float32
    u32 = u.astype(f32).reshape(bsz, s, SSM_GROUPS, SSM_GROUP_DIM)
    dt = jnp.exp(log_dt.astype(f32))[:, None]
    ar = a_re.astype(f32)
    ai = a_im.astype(f32)
    mag = jnp.exp(ar * dt)
    ang = ai * dt
    abar_re = mag * jnp.cos(ang)
    abar_im = mag * jnp.sin(ang)
    den = ar * ar + ai * ai
    nr = abar_re - 1.0
    ni = abar_im
    k_re = (nr * ar + ni * ai) / den
    k_im = (ni * ar - nr * ai) / den
    br = b_re.astype(f32)
    bi = b_im.astype(f32)
    bb_re = k_re[..., None] * br - k_im[..., None] * bi
    bb_im = k_re[..., None] * bi + k_im[..., None] * br
    bu_re = jnp.einsum('bsgh,gph->bsgp', u32, bb_re)
    bu_im = jnp.einsum('bsgh,gph->bsgp', u32, bb_im)
    shape = bu_re.shape
    _, _, x_re, x_im = lax.associative_scan(
        _scan_combine,
        (jnp.broadcast_to(abar_re, shape), jnp.broadcast_to(abar_im, shape), bu_re, bu_im),
        axis=1)
    y = (jnp.einsum('bsgp,ghp->bsgh', x_re, c_re.astype(f32))
         - jnp.einsum('bsgp,ghp->bsgh', x_im, c_im.astype(f32)))
    y = y.reshape(bsz, s, SSM_WIDTH) + d_skip.astype(f32) * u32.reshape(bsz, s, SSM_WIDTH)
    gv = jnp.einsum('bsc,ce->bse', y, w_glu.astype(f32))
    val, gate = jnp.split(gv, 2, axis=-1)
    return (val * jax.nn.sigmoid(gate)).astype(u.dtype)

def _even_mixer(h, w_in, pool_w, pool_scale, log_dt, a_re, a_im, b_re, b_im,
                c_re, c_im, d_skip, w_glu, w_out):
    proj = jnp.einsum('bsd,de->bse', h, w_in)
    u_pool = proj[..., :POOL_WIDTH]
    u_ssm = proj[..., POOL_WIDTH:MIX_WIDTH]
    z = proj[..., MIX_WIDTH:]
    y_pool = _multiscale_pool(u_pool, pool_w, pool_scale)
    y_ssm = _s5(u_ssm, log_dt, a_re, a_im, b_re, b_im, c_re, c_im, d_skip, w_glu)
    y = jnp.concatenate([y_pool, y_ssm], axis=-1) * jax.nn.silu(z)
    return jnp.einsum('bse,ed->bsd', y, w_out)

def _odd_mixer(h, w_in, conv_w, conv_b, ln_g, ln_b, w_out):
    proj = jnp.einsum('bsd,de->bse', h, w_in)
    val = proj[..., :CONV_CHANNELS]
    gt = proj[..., CONV_CHANNELS:2 * CONV_CHANNELS]
    z = proj[..., 2 * CONV_CHANNELS:]
    g = (val * jax.nn.sigmoid(gt)).astype(jnp.float32)
    kern = conv_w.astype(jnp.float32)[:, None, :]
    c = lax.conv_general_dilated(
        g, kern, window_strides=(1,), padding=[(CONV_KERNEL - 1, 0)],
        dimension_numbers=('NWC', 'WIO', 'NWC'), feature_group_count=CONV_CHANNELS)
    c = c + conv_b.astype(jnp.float32)
    mu = jnp.mean(c, axis=-1, keepdims=True)
    cc = c - mu
    var = jnp.mean(cc * cc, axis=-1, keepdims=True)
    c = cc * lax.rsqrt(var + LN_EPS) * ln_g.astype(jnp.float32) + ln_b.astype(jnp.float32)
    y = (jax.nn.silu(c) * jax.nn.silu(z.astype(jnp.float32))).astype(h.dtype)
    return jnp.einsum('bse,ed->bsd', y, w_out)

def first_inputs(seed: int = 0) -> dict:
    key = jax.random.key(seed)
    ks = jax.random.split(key, 24)
    f32 = jnp.float32

    def nrm(k, shape, scale):
        return jax.random.normal(k, shape, f32) * scale

    n_idx = jnp.arange(SSM_STATE, dtype=f32)
    a_im0 = jnp.broadcast_to(math.pi * n_idx, (N_EVEN, SSM_GROUPS, SSM_STATE))
    return {
        "x": jax.random.normal(ks[0], (BATCH, SEQ, D_MODEL), f32),
        "even_norm": 1.0 + nrm(ks[1], (N_EVEN, D_MODEL), 0.05),
        "even_w_in": nrm(ks[2], (N_EVEN, D_MODEL, 2 * MIX_WIDTH), D_MODEL ** -0.5),
        "pool_w": nrm(ks[3], (N_EVEN, POOL_GROUPS, POOL_GROUP_DIM, POOL_GROUP_DIM), POOL_GROUP_DIM ** -0.5),
        "pool_scale": 1.0 + nrm(ks[4], (N_EVEN, POOL_WIDTH), 0.05),
        "ssm_log_dt": jax.random.uniform(ks[5], (N_EVEN, SSM_GROUPS), f32,
                                         math.log(DT_MIN), math.log(DT_MAX)),
        "ssm_a_re": -0.5 * jnp.exp(nrm(ks[6], (N_EVEN, SSM_GROUPS, SSM_STATE), 0.05)),
        "ssm_a_im": a_im0 + nrm(ks[7], (N_EVEN, SSM_GROUPS, SSM_STATE), 0.01),
        "ssm_b_re": nrm(ks[8], (N_EVEN, SSM_GROUPS, SSM_STATE, SSM_GROUP_DIM), (2 * SSM_GROUP_DIM) ** -0.5),
        "ssm_b_im": nrm(ks[9], (N_EVEN, SSM_GROUPS, SSM_STATE, SSM_GROUP_DIM), (2 * SSM_GROUP_DIM) ** -0.5),
        "ssm_c_re": nrm(ks[10], (N_EVEN, SSM_GROUPS, SSM_GROUP_DIM, SSM_STATE), SSM_STATE ** -0.5),
        "ssm_c_im": nrm(ks[11], (N_EVEN, SSM_GROUPS, SSM_GROUP_DIM, SSM_STATE), SSM_STATE ** -0.5),
        "ssm_d": nrm(ks[12], (N_EVEN, SSM_WIDTH), 1.0),
        "ssm_w_glu": nrm(ks[13], (N_EVEN, SSM_WIDTH, 2 * SSM_WIDTH), SSM_WIDTH ** -0.5),
        "even_w_out": nrm(ks[14], (N_EVEN, MIX_WIDTH, D_MODEL), MIX_WIDTH ** -0.5),
        "odd_norm": 1.0 + nrm(ks[15], (N_ODD, D_MODEL), 0.05),
        "odd_w_in": nrm(ks[16], (N_ODD, D_MODEL, 3 * CONV_CHANNELS), D_MODEL ** -0.5),
        "conv_w": nrm(ks[17], (N_ODD, CONV_KERNEL, CONV_CHANNELS), CONV_KERNEL ** -0.5),
        "conv_b": nrm(ks[18], (N_ODD, CONV_CHANNELS), 0.02),
        "conv_ln_g": 1.0 + nrm(ks[19], (N_ODD, CONV_CHANNELS), 0.05),
        "conv_ln_b": nrm(ks[20], (N_ODD, CONV_CHANNELS), 0.02),
        "odd_w_out": nrm(ks[21], (N_ODD, CONV_CHANNELS, D_MODEL), CONV_CHANNELS ** -0.5),
        "final_norm": 1.0 + nrm(ks[22], (D_MODEL,), 0.05),
    }

def first_block(x, even_norm, even_w_in, pool_w, pool_scale, ssm_log_dt, ssm_a_re, ssm_a_im,
              ssm_b_re, ssm_b_im, ssm_c_re, ssm_c_im, ssm_d, ssm_w_glu, even_w_out,
              odd_norm, odd_w_in, conv_w, conv_b, conv_ln_g, conv_ln_b, odd_w_out, final_norm):
    for i in range(DEPTH):
        j = i // 2
        if i % 2 == 0:
            h = _rmsnorm(x, even_norm[j])
            x = x + _even_mixer(h, even_w_in[j], pool_w[j], pool_scale[j], ssm_log_dt[j],
                                ssm_a_re[j], ssm_a_im[j], ssm_b_re[j], ssm_b_im[j],
                                ssm_c_re[j], ssm_c_im[j], ssm_d[j], ssm_w_glu[j], even_w_out[j])
        else:
            h = _rmsnorm(x, odd_norm[j])
            x = x + _odd_mixer(h, odd_w_in[j], conv_w[j], conv_b[j], conv_ln_g[j],
                               conv_ln_b[j], odd_w_out[j])
    return _rmsnorm(x, final_norm)


HEAD_DIM = 64
D_FF = 2816
ROPE_THETA = 10000.0
NORM_EPS = 1e-6
NEG_INF = -1e30

A_HEADS = 4
A_VDIM = 2 * HEAD_DIM
A_OUT = A_HEADS * A_VDIM
A_QBLOCK = 128
A_SIZES = (2 * A_HEADS * HEAD_DIM, 2 * A_HEADS * HEAD_DIM, A_OUT)
A_COLS = sum(A_SIZES)

B_HEADS = 8
B_DIM = B_HEADS * HEAD_DIM
B_W_RANK = 64
B_A_RANK = 64
B_G_RANK = 128
B_GN_EPS = 64e-5
B_SIZES = (B_DIM, B_DIM, B_DIM, B_W_RANK, B_A_RANK, B_G_RANK)
B_COLS = sum(B_SIZES)
AB_COLS = A_COLS + B_COLS

C_HEADS = 8
C_KV_GROUPS = 2
C_HPG = C_HEADS // C_KV_GROUPS
C_OUT = C_HEADS * HEAD_DIM
C_KVW = C_KV_GROUPS * HEAD_DIM
CMP_BLOCK = 32
CMP_STRIDE = 16
CMP_HIDDEN = 256
SLC_BLOCK = 64
N_SELECT = 16
WINDOW = 512
C_QBLOCK = 64
FORCE_BONUS = 1e4
C_SIZES = (C_OUT, C_KVW, C_KVW, C_KVW, C_KVW, C_KVW, C_KVW, 3 * C_HEADS)
C_COLS = sum(C_SIZES)

D_HEADS = 4
D_QK = 64
D_V = 128
D_OUT = D_HEADS * D_V
D_CHUNK = 64
D_CONV = 4
D_SIZES = (D_HEADS * D_QK, D_HEADS * D_QK, D_OUT, D_HEADS, D_HEADS, D_OUT)
D_COLS = sum(D_SIZES)
CD_COLS = C_COLS + D_COLS


def rmsnorm(x, w, eps=NORM_EPS):
    xf = x.astype(jnp.float32)
    y = xf * lax.rsqrt(jnp.mean(xf * xf, axis=-1, keepdims=True) + eps)
    return (y * w.astype(jnp.float32)).astype(x.dtype)

def split_cols(p, sizes):
    return jnp.split(p, [int(c) for c in np.cumsum(sizes)[:-1]], axis=-1)

def rope_tables(pos):
    inv = jnp.asarray(ROPE_THETA ** (-np.arange(0, HEAD_DIM, 2, dtype=np.float32) / HEAD_DIM), jnp.float32)
    ang = pos[:, None] * inv[None, :]
    ang = jnp.concatenate([ang, ang], axis=-1)
    return jnp.cos(ang), jnp.sin(ang)

def apply_rope(x, cos, sin):
    x1, x2 = jnp.split(x, 2, axis=-1)
    rot = jnp.concatenate([-x2, x1], axis=-1)
    return (x * cos + rot * sin).astype(x.dtype)

def swiglu(x, wg, wu, wd):
    return (jax.nn.silu(x @ wg) * (x @ wu)) @ wd

def lambda_init(layer):
    return 0.8 - 0.6 * math.exp(-0.3 * layer)

def diff_attention(qa, ka, va, lam, subln_w, lam_init, cos, sin):
    B, T, _ = qa.shape
    q = apply_rope(qa.reshape(B, T, A_HEADS, 2, HEAD_DIM).transpose(0, 2, 3, 1, 4), cos, sin) * (HEAD_DIM ** -0.5)
    k = apply_rope(ka.reshape(B, T, A_HEADS, 2, HEAD_DIM).transpose(0, 2, 3, 1, 4), cos, sin)
    v = va.reshape(B, T, A_HEADS, A_VDIM).transpose(0, 2, 1, 3)
    lam32 = lam.astype(jnp.float32)
    lam_full = jnp.exp(jnp.sum(lam32[0] * lam32[1])) - jnp.exp(jnp.sum(lam32[2] * lam32[3])) + lam_init
    nb = T // A_QBLOCK
    qb = q.reshape(B, A_HEADS, 2, nb, A_QBLOCK, HEAD_DIM).transpose(3, 0, 1, 2, 4, 5)
    kpos = jnp.arange(T)

    def block(args):
        qi, i = args
        s = jnp.einsum('bhcqd,bhckd->bhcqk', qi, k).astype(jnp.float32)
        qpos = i * A_QBLOCK + jnp.arange(A_QBLOCK)
        mask = kpos[None, :] <= qpos[:, None]
        p = jax.nn.softmax(jnp.where(mask, s, NEG_INF), axis=-1)
        attn = p[:, :, 0] - lam_full * p[:, :, 1]
        return jnp.einsum('bhqk,bhke->bhqe', attn.astype(v.dtype), v)

    o = lax.map(block, (qb, jnp.arange(nb)))
    o = o.transpose(1, 0, 3, 2, 4).reshape(B, T, A_HEADS, A_VDIM)
    o = rmsnorm(o, subln_w) * (1.0 - lam_init)
    return o.reshape(B, T, A_OUT)

def rwkv7_time_mix(p, mu, w0, w2, a0, a2, g2, k_k, k_a, r_k, ln_w, ln_b):
    B, T, _ = p.shape
    prev = jnp.pad(p[:, :-1], ((0, 0), (1, 0), (0, 0)))
    xm = p + (prev - p) * mu
    r, k, v, wl, al, gl = split_cols(xm, B_SIZES)
    w = -jax.nn.softplus(-(w0 + jnp.tanh(wl) @ w2)) - 0.5
    a = jax.nn.sigmoid(a0 + al @ a2)
    g = jax.nn.sigmoid(gl) @ g2

    def heads(z):
        return z.reshape(B, T, B_HEADS, HEAD_DIM).astype(jnp.float32)

    kk = heads(k * k_k)
    kk = kk * lax.rsqrt(jnp.sum(kk * kk, axis=-1, keepdims=True) + 1e-12)
    k = k * (1.0 + (a - 1.0) * k_a)
    r_h, k_h, v_h, a_h = heads(r), heads(k), heads(v), heads(a)
    decay = jnp.exp(-jnp.exp(heads(w)))

    def step(S, inp):
        r_t, w_t, k_t, v_t, kk_t, a_t = inp
        S = (S * w_t[:, :, None, :]
             - jnp.einsum('bhvk,bhk->bhv', S, kk_t)[..., None] * (kk_t * a_t)[:, :, None, :]
             + v_t[..., None] * k_t[:, :, None, :])
        return S, jnp.einsum('bhvk,bhk->bhv', S, r_t)

    def tm(z):
        return z.transpose(1, 0, 2, 3)

    S0 = jnp.zeros((B, B_HEADS, HEAD_DIM, HEAD_DIM), jnp.float32)
    _, y = lax.scan(step, S0, (tm(r_h), tm(decay), tm(k_h), tm(v_h), tm(kk), tm(a_h)))
    y = y.transpose(1, 0, 2, 3)
    mean = jnp.mean(y, axis=-1, keepdims=True)
    var = jnp.mean(jnp.square(y - mean), axis=-1, keepdims=True)
    y = (y - mean) * lax.rsqrt(var + B_GN_EPS) * ln_w.reshape(B_HEADS, HEAD_DIM) + ln_b.reshape(B_HEADS, HEAD_DIM)
    bonus = jnp.sum(r_h * k_h * r_k, axis=-1, keepdims=True) * v_h
    out = (y + bonus).reshape(B, T, B_DIM).astype(p.dtype)
    return out * g

def compress_blocks(z, pe, w1, w2):
    B, G, T, d = z.shape
    n_cmp = (T - CMP_BLOCK) // CMP_STRIDE + 1
    idx = CMP_STRIDE * np.arange(n_cmp)[:, None] + np.arange(CMP_BLOCK)[None, :]
    blocks = (z[:, :, idx] + pe).reshape(B, G, n_cmp, CMP_BLOCK * d)
    return jax.nn.gelu(blocks @ w1) @ w2

def selection_map(n_cmp, n_slc):
    c0 = CMP_STRIDE * np.arange(n_cmp)[:, None]
    s0 = SLC_BLOCK * np.arange(n_slc)[None, :]
    shared = np.clip(np.minimum(c0 + CMP_BLOCK, s0 + SLC_BLOCK) - np.maximum(c0, s0), 0, None)
    return jnp.asarray(shared / CMP_BLOCK, jnp.float32)

def native_sparse_attention(q, kc, vc, ks, vs, kw, vw, gate_logits,
                            pe_k, w1_k, w2_k, pe_v, w1_v, w2_v, cos, sin):
    B, T, _ = q.shape
    dt = q.dtype
    q = apply_rope(q.reshape(B, T, C_KV_GROUPS, C_HPG, HEAD_DIM).transpose(0, 2, 3, 1, 4), cos, sin) * (HEAD_DIM ** -0.5)

    def groups(z):
        return z.reshape(B, T, C_KV_GROUPS, HEAD_DIM).transpose(0, 2, 1, 3)

    kc, vc, ks, vs, kw, vw = [groups(z) for z in (kc, vc, ks, vs, kw, vw)]
    ks = apply_rope(ks, cos, sin)
    kw = apply_rope(kw, cos, sin)
    n_cmp = (T - CMP_BLOCK) // CMP_STRIDE + 1
    cmp_end = CMP_STRIDE * np.arange(n_cmp) + CMP_BLOCK - 1
    ccos, csin = rope_tables(jnp.asarray(cmp_end, jnp.float32))
    k_cmp = apply_rope(compress_blocks(kc, pe_k, w1_k, w2_k), ccos, csin)
    v_cmp = compress_blocks(vc, pe_v, w1_v, w2_v)
    n_slc = T // SLC_BLOCK
    n_sel = min(N_SELECT, n_slc)
    sel_map = selection_map(n_cmp, n_slc)
    ks_blocks = ks.reshape(B, C_KV_GROUPS, n_slc, SLC_BLOCK, HEAD_DIM)
    vs_blocks = vs.reshape(B, C_KV_GROUPS, n_slc, SLC_BLOCK, HEAD_DIM)
    kw_pad = jnp.pad(kw, ((0, 0), (0, 0), (WINDOW, 0), (0, 0)))
    vw_pad = jnp.pad(vw, ((0, 0), (0, 0), (WINDOW, 0), (0, 0)))
    gates = jax.nn.sigmoid(gate_logits).reshape(B, T, C_KV_GROUPS, C_HPG, 3).transpose(0, 2, 3, 1, 4)
    b_idx = jnp.arange(B)[:, None, None, None]
    g_idx = jnp.arange(C_KV_GROUPS)[None, :, None, None]
    blk = jnp.arange(n_slc)
    cmp_end_j = jnp.asarray(cmp_end)

    def block(i):
        s0 = i * C_QBLOCK
        t = s0 + jnp.arange(C_QBLOCK)
        qi = lax.dynamic_slice_in_dim(q, s0, C_QBLOCK, axis=3)
        mc = cmp_end_j[None, :] <= t[:, None]
        sc = jnp.einsum('bghqd,bgnd->bghqn', qi, k_cmp).astype(jnp.float32)
        pc = jnp.where(mc, jax.nn.softmax(jnp.where(mc, sc, NEG_INF), axis=-1), 0.0)
        o_cmp = jnp.einsum('bghqn,bgne->bghqe', pc.astype(dt), v_cmp)
        imp = jnp.einsum('bghqn,nj->bgqj', pc, sel_map)
        cur = t // SLC_BLOCK
        forced = (blk[None, :] == 0) | (blk[None, :] == cur[:, None]) | (blk[None, :] == cur[:, None] - 1)
        valid = blk[None, :] * SLC_BLOCK <= t[:, None]
        score = jnp.where(valid, imp + jnp.where(forced, FORCE_BONUS, 0.0), NEG_INF)
        _, sel = lax.top_k(score, n_sel)
        kg = ks_blocks[b_idx, g_idx, sel]
        vg = vs_blocks[b_idx, g_idx, sel]
        pos = sel[..., None] * SLC_BLOCK + jnp.arange(SLC_BLOCK)
        ms = (pos <= t[:, None, None])[:, :, None]
        ss = jnp.where(ms, jnp.einsum('bghqd,bgqnkd->bghqnk', qi, kg).astype(jnp.float32), NEG_INF)
        ps = jax.nn.softmax(ss.reshape(B, C_KV_GROUPS, C_HPG, C_QBLOCK, -1), axis=-1).reshape(ss.shape)
        o_slc = jnp.einsum('bghqnk,bgqnke->bghqe', ps.astype(dt), vg)
        kwi = lax.dynamic_slice_in_dim(kw_pad, s0, C_QBLOCK + WINDOW, axis=2)
        vwi = lax.dynamic_slice_in_dim(vw_pad, s0, C_QBLOCK + WINDOW, axis=2)
        wpos = s0 - WINDOW + jnp.arange(C_QBLOCK + WINDOW)
        mw = (wpos[None, :] <= t[:, None]) & (wpos[None, :] > t[:, None] - WINDOW) & (wpos[None, :] >= 0)
        sw = jnp.einsum('bghqd,bgkd->bghqk', qi, kwi).astype(jnp.float32)
        pw = jax.nn.softmax(jnp.where(mw, sw, NEG_INF), axis=-1)
        o_win = jnp.einsum('bghqk,bgke->bghqe', pw.astype(dt), vwi)
        gi = lax.dynamic_slice_in_dim(gates, s0, C_QBLOCK, axis=3)
        return gi[..., 0:1] * o_cmp + gi[..., 1:2] * o_slc + gi[..., 2:3] * o_win

    o = lax.map(block, jnp.arange(T // C_QBLOCK))
    return o.transpose(1, 0, 4, 2, 3, 5).reshape(B, T, C_OUT)

def causal_conv(x, w, b):
    K, T = w.shape[0], x.shape[1]
    xp = jnp.pad(x, ((0, 0), (K - 1, 0), (0, 0)))
    return sum(xp[:, j:j + T] * w[j] for j in range(K)) + b

def mlstm(q, k, v, ig, fg, og, conv_w, conv_b, ig_b, fg_b, norm_w):
    B, T, _ = q.shape
    qk = jax.nn.silu(causal_conv(jnp.concatenate([q, k], axis=-1), conv_w, conv_b))
    q, k = qk[..., :D_HEADS * D_QK], qk[..., D_HEADS * D_QK:]
    nc = T // D_CHUNK

    def chunks(z, dim):
        return z.astype(jnp.float32).reshape(B, nc, D_CHUNK, D_HEADS, dim).transpose(1, 0, 3, 2, 4)

    def gate_chunks(z):
        return z.reshape(B, nc, D_CHUNK, D_HEADS).transpose(1, 0, 3, 2)

    qc = chunks(q, D_QK) * (D_QK ** -0.5)
    kc = chunks(k, D_QK)
    vc = chunks(v, D_V)
    li = gate_chunks((ig + ig_b).astype(jnp.float32))
    lf = gate_chunks(jax.nn.log_sigmoid((fg + fg_b).astype(jnp.float32)))
    causal = jnp.tril(jnp.ones((D_CHUNK, D_CHUNK), bool))

    def step(carry, inp):
        C, n, m = carry
        qs, ks, vs, lis, lfs = inp
        b = jnp.cumsum(lfs, axis=-1)
        dmat = jnp.where(causal, b[..., :, None] - b[..., None, :] + lis[..., None, :], -jnp.inf)
        m_s = jnp.maximum(b + m[..., None], jnp.max(dmat, axis=-1))
        carry_w = jnp.exp(b + m[..., None] - m_s)
        sqk = jnp.einsum('bhsd,bhrd->bhsr', qs, ks) * jnp.exp(dmat - m_s[..., None])
        num = carry_w[..., None] * jnp.einsum('bhsd,bhde->bhse', qs, C) + jnp.einsum('bhsr,bhre->bhse', sqk, vs)
        den = carry_w * jnp.einsum('bhsd,bhd->bhs', qs, n) + jnp.sum(sqk, axis=-1)
        h = num / jnp.maximum(jnp.abs(den), jnp.exp(-m_s))[..., None]
        b_last = b[..., -1]
        g = b_last[..., None] - b + lis
        m_new = jnp.maximum(b_last + m, jnp.max(g, axis=-1))
        decay_c = jnp.exp(b_last + m - m_new)
        wr = jnp.exp(g - m_new[..., None])
        C = decay_c[..., None, None] * C + jnp.einsum('bhr,bhrd,bhre->bhde', wr, ks, vs)
        n = decay_c[..., None] * n + jnp.einsum('bhr,bhrd->bhd', wr, ks)
        return (C, n, m_new), h

    init = (jnp.zeros((B, D_HEADS, D_QK, D_V), jnp.float32),
            jnp.zeros((B, D_HEADS, D_QK), jnp.float32),
            jnp.zeros((B, D_HEADS), jnp.float32))
    _, h = lax.scan(step, init, (qc, kc, vc, li, lf))
    h = h.transpose(1, 0, 3, 2, 4).reshape(B, T, D_HEADS, D_V)
    h = rmsnorm(h, norm_w.reshape(D_HEADS, D_V)).reshape(B, T, D_OUT)
    return h.astype(og.dtype) * jax.nn.sigmoid(og)

def second_inputs(seed: int = 0) -> dict:
    key = jax.random.key(seed)
    keys = iter(jax.random.split(key, 48))

    def nrm(shape, scale):
        return jax.random.normal(next(keys), shape, jnp.float32) * scale

    def gain(shape):
        return 1.0 + nrm(shape, 0.02)

    L, E, O = DEPTH, (DEPTH + 1) // 2, DEPTH // 2
    d, f = D_MODEL, D_FF
    return {
        'x': nrm((BATCH, SEQ, d), 1.0),
        'ffa_norm': gain((L, d)),
        'ffa_gate': nrm((L, d, f), d ** -0.5),
        'ffa_up': nrm((L, d, f), d ** -0.5),
        'ffa_down': nrm((L, f, d), f ** -0.5),
        'mix_norm': gain((L, d)),
        'ffb_norm': gain((L, d)),
        'ffb_gate': nrm((L, d, f), d ** -0.5),
        'ffb_up': nrm((L, d, f), d ** -0.5),
        'ffb_down': nrm((L, f, d), f ** -0.5),
        'ab_w_in': nrm((E, d, AB_COLS), d ** -0.5),
        'ab_w_out': nrm((E, A_OUT + B_DIM, d), (A_OUT + B_DIM) ** -0.5),
        'diff_lam': nrm((E, 4, HEAD_DIM), 0.1),
        'diff_subln': gain((E, A_VDIM)),
        'rwkv_mu': jax.random.uniform(next(keys), (E, B_COLS), jnp.float32),
        'rwkv_w0': jnp.linspace(-6.0, 1.0, B_DIM, dtype=jnp.float32)[None, :] + nrm((E, B_DIM), 0.1),
        'rwkv_w2': nrm((E, B_W_RANK, B_DIM), B_W_RANK ** -0.5),
        'rwkv_a0': nrm((E, B_DIM), 0.1),
        'rwkv_a2': nrm((E, B_A_RANK, B_DIM), B_A_RANK ** -0.5),
        'rwkv_g2': nrm((E, B_G_RANK, B_DIM), B_G_RANK ** -0.5),
        'rwkv_kk': 0.85 + nrm((E, B_DIM), 0.05),
        'rwkv_ka': 1.0 + nrm((E, B_DIM), 0.05),
        'rwkv_rk': nrm((E, B_HEADS, HEAD_DIM), 0.1),
        'rwkv_lnw': gain((E, B_DIM)),
        'rwkv_lnb': nrm((E, B_DIM), 0.02),
        'cd_w_in': nrm((O, d, CD_COLS), d ** -0.5),
        'cd_w_out': nrm((O, C_OUT + D_OUT, d), (C_OUT + D_OUT) ** -0.5),
        'nsa_pe_k': nrm((O, CMP_BLOCK, HEAD_DIM), 0.1),
        'nsa_w1_k': nrm((O, CMP_BLOCK * HEAD_DIM, CMP_HIDDEN), (CMP_BLOCK * HEAD_DIM) ** -0.5),
        'nsa_w2_k': nrm((O, CMP_HIDDEN, HEAD_DIM), CMP_HIDDEN ** -0.5),
        'nsa_pe_v': nrm((O, CMP_BLOCK, HEAD_DIM), 0.1),
        'nsa_w1_v': nrm((O, CMP_BLOCK * HEAD_DIM, CMP_HIDDEN), (CMP_BLOCK * HEAD_DIM) ** -0.5),
        'nsa_w2_v': nrm((O, CMP_HIDDEN, HEAD_DIM), CMP_HIDDEN ** -0.5),
        'mlstm_conv_w': nrm((O, D_CONV, 2 * D_HEADS * D_QK), 0.5),
        'mlstm_conv_b': nrm((O, 2 * D_HEADS * D_QK), 0.02),
        'mlstm_ig_b': -2.0 + nrm((O, D_HEADS), 0.1),
        'mlstm_fg_b': jnp.linspace(3.0, 6.0, D_HEADS, dtype=jnp.float32)[None, :] + nrm((O, D_HEADS), 0.1),
        'mlstm_norm': gain((O, D_OUT)),
        'final_norm': gain((d,)),
    }

def second_block(x, ffa_norm, ffa_gate, ffa_up, ffa_down, mix_norm, ffb_norm, ffb_gate, ffb_up, ffb_down,
              ab_w_in, ab_w_out, diff_lam, diff_subln,
              rwkv_mu, rwkv_w0, rwkv_w2, rwkv_a0, rwkv_a2, rwkv_g2, rwkv_kk, rwkv_ka, rwkv_rk, rwkv_lnw, rwkv_lnb,
              cd_w_in, cd_w_out, nsa_pe_k, nsa_w1_k, nsa_w2_k, nsa_pe_v, nsa_w1_v, nsa_w2_v,
              mlstm_conv_w, mlstm_conv_b, mlstm_ig_b, mlstm_fg_b, mlstm_norm, final_norm):
    T = x.shape[1]
    cos, sin = rope_tables(jnp.arange(T, dtype=jnp.float32))
    for layer in range(DEPTH):
        j = layer // 2
        x = x + 0.5 * swiglu(rmsnorm(x, ffa_norm[layer]), ffa_gate[layer], ffa_up[layer], ffa_down[layer])
        h = rmsnorm(x, mix_norm[layer])
        if layer % 2 == 0:
            p = h @ ab_w_in[j]
            qa, ka, va = split_cols(p[..., :A_COLS], A_SIZES)
            oa = diff_attention(qa, ka, va, diff_lam[j], diff_subln[j], lambda_init(layer), cos, sin)
            ob = rwkv7_time_mix(p[..., A_COLS:], rwkv_mu[j], rwkv_w0[j], rwkv_w2[j], rwkv_a0[j], rwkv_a2[j],
                                rwkv_g2[j], rwkv_kk[j], rwkv_ka[j], rwkv_rk[j], rwkv_lnw[j], rwkv_lnb[j])
            mix = jnp.concatenate([oa, ob], axis=-1) @ ab_w_out[j]
        else:
            p = h @ cd_w_in[j]
            cq, ckc, cvc, cks, cvs, ckw, cvw, cg = split_cols(p[..., :C_COLS], C_SIZES)
            dq, dk, dv, di, df, dog = split_cols(p[..., C_COLS:], D_SIZES)
            oc = native_sparse_attention(cq, ckc, cvc, cks, cvs, ckw, cvw, cg,
                                         nsa_pe_k[j], nsa_w1_k[j], nsa_w2_k[j],
                                         nsa_pe_v[j], nsa_w1_v[j], nsa_w2_v[j], cos, sin)
            od = mlstm(dq, dk, dv, di, df, dog, mlstm_conv_w[j], mlstm_conv_b[j],
                       mlstm_ig_b[j], mlstm_fg_b[j], mlstm_norm[j])
            mix = jnp.concatenate([oc, od], axis=-1) @ cd_w_out[j]
        x = x + mix
        x = x + 0.5 * swiglu(rmsnorm(x, ffb_norm[layer]), ffb_gate[layer], ffb_up[layer], ffb_down[layer])
    return rmsnorm(x, final_norm)


def setup_inputs(seed=0):
    out = dict(first_inputs(seed))
    for name, value in second_inputs(seed + 1).items():
        if name != "x":
            out[name + "_2"] = value
    return out


def reference(
    x, even_norm, even_w_in, pool_w, pool_scale, ssm_log_dt, ssm_a_re, ssm_a_im, ssm_b_re,
    ssm_b_im, ssm_c_re, ssm_c_im, ssm_d, ssm_w_glu, even_w_out, odd_norm, odd_w_in, conv_w,
    conv_b, conv_ln_g, conv_ln_b, odd_w_out, final_norm, ffa_norm_2, ffa_gate_2, ffa_up_2,
    ffa_down_2, mix_norm_2, ffb_norm_2, ffb_gate_2, ffb_up_2, ffb_down_2, ab_w_in_2, ab_w_out_2,
    diff_lam_2, diff_subln_2, rwkv_mu_2, rwkv_w0_2, rwkv_w2_2, rwkv_a0_2, rwkv_a2_2, rwkv_g2_2,
    rwkv_kk_2, rwkv_ka_2, rwkv_rk_2, rwkv_lnw_2, rwkv_lnb_2, cd_w_in_2, cd_w_out_2, nsa_pe_k_2,
    nsa_w1_k_2, nsa_w2_k_2, nsa_pe_v_2, nsa_w1_v_2, nsa_w2_v_2, mlstm_conv_w_2, mlstm_conv_b_2,
    mlstm_ig_b_2, mlstm_fg_b_2, mlstm_norm_2, final_norm_2,
):
    x = first_block(
        x, even_norm, even_w_in, pool_w, pool_scale, ssm_log_dt, ssm_a_re, ssm_a_im, ssm_b_re,
        ssm_b_im, ssm_c_re, ssm_c_im, ssm_d, ssm_w_glu, even_w_out, odd_norm, odd_w_in, conv_w,
        conv_b, conv_ln_g, conv_ln_b, odd_w_out, final_norm,
    )
    return second_block(
        x, ffa_norm_2, ffa_gate_2, ffa_up_2, ffa_down_2, mix_norm_2, ffb_norm_2, ffb_gate_2,
        ffb_up_2, ffb_down_2, ab_w_in_2, ab_w_out_2, diff_lam_2, diff_subln_2, rwkv_mu_2,
        rwkv_w0_2, rwkv_w2_2, rwkv_a0_2, rwkv_a2_2, rwkv_g2_2, rwkv_kk_2, rwkv_ka_2, rwkv_rk_2,
        rwkv_lnw_2, rwkv_lnb_2, cd_w_in_2, cd_w_out_2, nsa_pe_k_2, nsa_w1_k_2, nsa_w2_k_2,
        nsa_pe_v_2, nsa_w1_v_2, nsa_w2_v_2, mlstm_conv_w_2, mlstm_conv_b_2, mlstm_ig_b_2,
        mlstm_fg_b_2, mlstm_norm_2, final_norm_2,
    )


_drawn_inputs = setup_inputs


def setup_inputs(seed=0):
    import zlib

    import numpy as np

    out = dict(_drawn_inputs(seed))
    spreads = {}
    factors = {'ssm_a_re': 64.0,
     'conv_ln_b': 4.896,
     'ffa_norm_2': 4.165,
     'ffb_norm_2': 5.979,
     'diff_subln_2': 21.805,
     'rwkv_a0_2': 3.754,
     'rwkv_kk_2': 5.02,
     'rwkv_ka_2': 2.889,
     'rwkv_lnw_2': 33.538,
     'rwkv_lnb_2': 34.207,
     'nsa_pe_k_2': 64.0,
     'nsa_pe_v_2': 34.576,
     'mlstm_conv_b_2': 64.0,
     'mlstm_ig_b_2': 64.0,
     'mlstm_norm_2': 64.0,
     'final_norm_2': 7.474,
     'ssm_b_re': 2.973,
     'ssm_b_im': 2.998,
     'ssm_c_re': 2.967,
     'ssm_c_im': 2.964,
     'cd_w_in_2': 4.65,
     'cd_w_out_2': 3.624,
     'nsa_w1_k_2': 8.0,
     'nsa_w2_k_2': 8.0,
     'nsa_w1_v_2': 5.131,
     'nsa_w2_v_2': 3.847,
     'mlstm_conv_w_2': 8.0,
     'mlstm_fg_b_2': 8.0}
    for name, (base, spread) in spreads.items():
        noise = np.random.default_rng([zlib.crc32(name.encode()), seed]).standard_normal(out[name].shape)
        drawn = base * np.exp(spread * noise) if base else spread * noise
        out[name] = jnp.asarray(drawn.astype(out[name].dtype))
    for name, factor in factors.items():
        out[name] = (out[name] * factor).astype(out[name].dtype)
    return out
```

```python
from contextlib import ExitStack
import math

import numpy as np

import concourse.bass as bass
from concourse import mybir

F32 = mybir.dt.float32
I32 = mybir.dt.int32
ACT = mybir.ActivationFunctionType
ALU = mybir.AluOpType
AX = mybir.AxisListType.X
MUL, ADD, SUB, MAX, MIN = ALU.mult, ALU.add, ALU.subtract, ALU.max, ALU.min

P = 128
T = 512
NT = T // P
SLOT = 1408
NSLOT = 8
FF = 22
LAM0 = 0.8 - 0.6 * math.exp(-0.3 * 0)
DECAY = math.exp(-0.5)
NEG = -1e30

COLS = [
    ("even_norm", 8), ("pool_scale", 4), ("ssm_d", 4), ("log_dt", 16), ("a_re", 16), ("a_im", 16),
    ("odd_norm", 8), ("conv_w", 248), ("conv_b", 8), ("ln_g", 8), ("ln_b", 8), ("final_norm", 8),
    ("ffa_norm", 16), ("mix_norm", 16), ("ffb_norm", 16), ("mu", 14), ("w0", 4), ("a0", 4),
    ("kk", 4), ("ka", 4), ("rk", 4), ("lnw", 4), ("lnb", 4), ("subln", 1), ("mconv_w", 16),
    ("mconv_b", 4), ("gate_b", 1), ("mnorm", 4), ("final_norm_2", 8), ("lam", 256),
    ("pe_k", 16), ("pe_v", 16),
]
COL, NCOL = {}, 0
for _name, _n in COLS:
    COL[_name] = NCOL
    NCOL += _n

CONSTS = [
    ("ident", 128), ("ones", 128), ("bones", 128), ("rot", 128), ("cos", 512), ("sin", 512),
    ("ccos", 31), ("csin", 31), ("negmask", 128), ("cmpmask", 4 * 31), ("cmprow", 4),
    ("ml", 384), ("nstrict", 128), ("cm", 4), ("ncm", 4), ("scanm", 512), ("triu", 128),
    ("ident64", 64), ("eye32", 1024), ("sel", 512), ("invpos", 64),
]
CC, NCONST = {}, 0
for _name, _n in CONSTS:
    CC[_name] = NCONST
    NCONST += _n


class Lane:

    def __init__(self, sem, chained):
        self.sem, self.chained = sem, chained
        self.ops, self.n, self.seen = [], 0, {}

    def wait(self, *marks):
        for m in marks:
            if m is None:
                continue
            if isinstance(m, list):
                self.wait(*m)
                continue
            sem, value = m
            if self.seen.get(sem.name, 0) < value:
                self.seen[sem.name] = value
                self.ops.append(lambda e, s=sem, v=value: e.wait_ge(s, v))

    def do(self, fn, *after):
        if self.chained and self.n:
            self.wait((self.sem, self.n))
        self.wait(*after)
        self.n += 1
        self.ops.append(lambda e, s=self.sem: fn(e).then_inc(s, 1))
        return (self.sem, self.n)

    def plain(self, fn):
        self.ops.append(fn)

    def last(self):
        return (self.sem, self.n) if self.n else None

    def play(self, e):
        for op in self.ops:
            op(e)


class DmaSem:
    def __init__(self, sem):
        self.sem, self.n = sem, 0

    def start(self, lane, out, in_, *after):
        lane.wait(*after)
        self.n += 16
        lane.plain(lambda e, o=out, i=in_, s=self.sem: e.dma_start(o, i).then_inc(s, 16))
        return (self.sem, self.n)


class Free(dict):
    pass


class Ring:

    def __init__(self, bufs):
        self.bufs, self.free, self.at = bufs, Free((i, None) for i in range(len(bufs))), 0

    def take(self):
        while self.at % len(self.bufs) not in self.free:
            self.at += 1
        i = self.at % len(self.bufs)
        self.at += 1
        return i, self.bufs[i], self.free.pop(i)


def build(nc, io):
    ctx = ExitStack()
    with ctx:
        sem = lambda n: ctx.enter_context(nc.semaphore(n))
        pe = Lane(sem("s_pe"), False)
        dv = Lane(sem("s_dve"), True)
        ac = Lane(sem("s_act"), True)
        po = Lane(sem("s_pool"), True)
        sp = Lane(sem("s_sp"), False)
        lanes = [pe, dv, ac, po]

        x = ctx.enter_context(nc.sbuf_tensor("x", [P, 8, T], F32))
        h = ctx.enter_context(nc.sbuf_tensor("h", [P, 8, T], F32))
        wr = ctx.enter_context(nc.sbuf_tensor("wr", [P, NSLOT, SLOT], F32))
        prm = ctx.enter_context(nc.sbuf_tensor("prm", [P, NCOL], F32))
        cst = ctx.enter_context(nc.sbuf_tensor("cst", [P, NCONST], F32))
        AREA = 27800
        area = ctx.enter_context(nc.sbuf_tensor("area", [P, AREA], F32))
        ps = ctx.enter_context(nc.psum_tensor("ps", [P, 8, 512], F32))

        top = [0]

        def alloc(n):
            a = top[0]
            top[0] += n
            assert top[0] <= AREA, top[0]
            return area[:, a:a + n]

        def tiles(k, n=T):
            return alloc(k * n).rearrange("p (k n) -> p k n", k=k)

        def pc(name, i=0, n=1):
            return prm[:, COL[name] + i:COL[name] + i + n]

        def cc(name, i=0, n=None):
            w = dict(CONSTS)[name] if n is None else n
            return cst[:, CC[name] + i:CC[name] + i + w]

        scratch = [nc.dram_tensor(f"scratch{i}", (4, 32, 32, 32), F32, kind="Internal").ap() for i in range(2)]
        ident, ones, bones = cc("ident"), cc("ones"), cc("bones")
        banks = Ring([ps[:, i, :] for i in range(8)])
        slots = Ring([wr[:, i, :] for i in range(NSLOT)])
        wsem = [DmaSem(sem(f"s_w{i}")) for i in range(NSLOT)]

        n_in = [0]

        def load(dst, src, *after):
            n_in[0] += 1
            return DmaSem(sem(f"s_in{n_in[0]}")).start(ac, dst, src, *after)

        s_x = DmaSem(sem("s_x"))
        s_sh = DmaSem(sem("s_sh"))
        s_out = DmaSem(sem("s_out"))
        s_c = DmaSem(sem("s_c"))

        def tt(ln, out, a, b, op, *after):
            return ln.do(lambda e: e.tensor_tensor(out, a, b, op), *after)

        def ts(ln, out, a, s1, s2, o0, o1, *after):
            if o1 is None:
                return ln.do(lambda e: e.tensor_scalar(out, a, s1, None, o0), *after)
            return ln.do(lambda e: e.tensor_scalar(out, a, s1, s2, o0, o1), *after)

        def stt(out, a, s, b, o0, o1, *after):
            return dv.do(lambda e: e.scalar_tensor_tensor(out=out, in0=a, scalar=s, in1=b, op0=o0, op1=o1),
                         *after)

        def copy(ln, out, a, *after):
            return ln.do(lambda e: e.tensor_copy(out, a), *after)

        def act(out, a, f, *after, **kw):
            return ac.do(lambda e: e.activation(out, a, f, **kw), *after)

        def recip(out, a, *after):
            return dv.do(lambda e: e.reciprocal(out, a), *after)

        def memset(ln, out, v, *after):
            return ln.do(lambda e: e.memset(out, v), *after)

        def mm(out, l, r, start, stop, mark=False):
            f = lambda e: e.matmul(out, l, r, start=start, stop=stop, skip_group_check=True)
            return pe.do(f) if mark else pe.plain(f)

        def tr(out, in_, mark=False):
            k = in_.shape[0]
            f = lambda e: e.transpose(out, in_, ident[0:k, 0:k])
            return pe.do(f) if mark else pe.plain(f)

        def barrier():
            marks = [l.last() for l in lanes]
            for l in lanes:
                l.wait(*marks)
            return marks

        def bank():
            i, ap, free = banks.take()
            pe.wait(free)
            return i, ap

        def wload(src, n, *after):
            i, ap, free = slots.take()
            mark = wsem[i].start(sp, ap[:, 0:n], src, free, *after)
            return i, ap, mark

        m_c = s_c.start(ac, cst[:, :], io["consts"])
        m_p = load(prm[:, :], io["params"])
        m_x = s_x.start(sp, x[:, :, :], io["x"])
        for l in lanes:
            l.wait(m_c, m_p)
        dv.wait(m_x)
        ac.wait(m_x)
        po.wait(m_x)

        def linear(xs, w, n_out, kt, evac, after=(), first=0):
            pe.wait(*after)
            per = 8 if kt == 8 else (11 if kt == 22 else kt)
            for o in range(n_out):
                b, acc = bank()
                k = 0
                while k < kt:
                    s, ap, mark = wload(w[first + o, :, k * P:(k + per) * P], per * P)
                    pe.wait(mark)
                    for j in range(per):
                        end = k + j == kt - 1
                        done = mm(acc, ap[:, j * P:(j + 1) * P], xs[k + j], k + j == 0, end,
                                  mark=(j == per - 1))
                    slots.free[s] = done
                    k += per
                banks.free[b] = evac(o, acc, done)

        def linear_tok(xs, w, n, evac, after=()):
            pe.wait(*after)
            bs = [bank() for _ in range(NT)]
            for k in range(8):
                s, ap, mark = wload(w[k], n)
                pe.wait(mark)
                for t in range(NT):
                    done = mm(bs[t][1][:, 0:n], xs[k][:, t * P:(t + 1) * P], ap[:, 0:n], k == 0, k == 7,
                              mark=(t == NT - 1))
                slots.free[s] = done
            for t in range(NT):
                banks.free[bs[t][0]] = evac(t, bs[t][1][:, 0:n], done)

        def rstd_of(acc, out, scale, eps, done):
            m = ts(dv, out, acc, scale, eps, MUL, ADD, done)
            free = m
            m = recip(out, out)
            return act(out, out, ACT.Sqrt, m), free

        def rmsnorm(src, dst, gain, eps, sq, rstd, *after):
            b, acc = bank()
            r = []
            for k in range(8):
                m = act(sq[k % 2], src[:, k, :], ACT.Square, *after, r[k - 2] if k >= 2 else None)
                pe.wait(m)
                r.append(mm(acc, ones, sq[k % 2], k == 0, k == 7, mark=True))
            m, banks.free[b] = rstd_of(acc, rstd, 1.0 / 1024, eps, r[-1])
            for k in range(8):
                last = stt(dst[:, k, :], src[:, k, :], gain(k), rstd, MUL, MUL, m)
            return last

        def hs(src=h):
            return [src[:, k, :] for k in range(8)]

        def swiglu(norm, i, wg, wu, wd):
            top[0] = 0
            sq, rstd = tiles(2), alloc(T)
            hid = tiles(FF)
            sg = tiles(2)
            m = rmsnorm(x, h, lambda k: pc(norm, 8 * i + k), 1e-6, [sq[:, 0, :], sq[:, 1, :]], rstd)
            pe.wait(m)
            state = {}

            def gate(o):
                b, acc = bank()
                s, ap, mark = wload(wg[i, o], 8 * P)
                pe.wait(mark)
                for k in range(8):
                    d = mm(acc, ap[:, k * P:(k + 1) * P], h[:, k, :], k == 0, k == 7, mark=(k == 7))
                slots.free[s] = d
                m = act(sg[:, o % 2, :], acc, ACT.Silu, d, state.get(o - 2))
                banks.free[b] = m
                return m

            for o in range(FF):
                mg = gate(o)
                b, acc = bank()
                s, ap, mark = wload(wu[i, o], 8 * P)
                pe.wait(mark)
                for k in range(8):
                    d = mm(acc, ap[:, k * P:(k + 1) * P], h[:, k, :], k == 0, k == 7, mark=(k == 7))
                slots.free[s] = d
                state[o] = tt(dv, hid[:, o, :], acc, sg[:, o % 2, :], MUL, d, mg)
                banks.free[b] = state[o]

            def add(o, acc, d):
                return stt(x[:, o, :], acc, 0.5, x[:, o, :], MUL, ADD, d)

            pe.wait(dv.last())
            linear([hid[:, k, :] for k in range(FF)], wd[i], 8, FF, add)
            barrier()

        def residual(o, acc, d):
            return tt(dv, x[:, o, :], acc, x[:, o, :], ADD, d)

        def even():
            top[0] = 0
            sq, rstd = tiles(2), alloc(T)
            y = tiles(8)
            us = tiles(4)
            HT = T // 2
            ct = alloc(16 * HT).rearrange("p (q t) -> p q t", q=16)
            st = alloc(16 * HT).rearrange("p (q t) -> p q t", q=16)
            small = alloc(24 * 16)

            def v(i):
                return small[:, i * 16:(i + 1) * 16]

            m_b = alloc(512)
            cw = alloc(2 * 512)
            cre, cim = cw[:, 0:512], cw[:, 512:1024]
            m_cl = load(cw, io["c_bd"])
            m_bl = load(m_b, io["b_re"])
            m_b2 = alloc(512)
            m_bl = load(m_b2, io["b_im"])
            hn = rmsnorm(x, h, lambda k: pc("even_norm", k), 1e-6, [sq[:, 0, :], sq[:, 1, :]], rstd)

            dt_, mag, co, si, kr, ki, t0, t1, t2, t3, t4, nr = [v(i) for i in range(12)]
            it = v(12).bitcast(I32)

            def exp_small(out, in_):
                ts(dv, t0, in_, 1.0 / math.log(2.0), None, MUL, None)
                ts(dv, t0, t0, -126.0, 126.0, MAX, MIN)
                ts(dv, t0, t0, 12582912.0, None, ADD, None)
                ts(dv, t0, t0, -12582912.0, None, ADD, None)
                stt(t1, t0, -0.693359375, in_, MUL, ADD)
                stt(t1, t0, 2.12194440e-4, t1, MUL, ADD)
                ts(dv, t1, t1, -0.7, 0.7, MAX, MIN)
                ts(dv, t2, t1, 1.0 / 5040, 1.0 / 720, MUL, ADD)
                for c in (1.0 / 120, 1.0 / 24, 1.0 / 6, 0.5, 1.0, 1.0):
                    tt(dv, t2, t2, t1, MUL)
                    ts(dv, t2, t2, c, None, ADD, None)
                ts(dv, it, t0, 127.0, 8388608.0, ADD, MUL)
                return tt(dv, out, t2, v(12), MUL)

            exp_small(dt_, pc("log_dt", 0, 16))
            tt(dv, t3, pc("a_re", 0, 16), dt_, MUL)
            exp_small(mag, t3)
            tt(dv, t3, pc("a_im", 0, 16), dt_, MUL)
            ts(dv, t0, t3, 1.0 / (2 * math.pi), 12582912.0, MUL, ADD)
            ts(dv, t0, t0, -12582912.0, None, ADD, None)
            stt(t3, t0, -6.28125, t3, MUL, ADD)
            stt(t3, t0, -(2 * math.pi - 6.28125), t3, MUL, ADD)
            m = ts(dv, t3, t3, 3.1415925, -3.1415925, MIN, MAX)
            act(si, t3, ACT.Sin, m)
            m = act(t4, t3, ACT.Abs)
            m = ts(dv, t4, t4, -1.0, math.pi / 2, MUL, ADD, m)
            m = act(co, t4, ACT.Sin, m)
            tt(dv, nr, mag, co, MUL, m)
            ts(dv, nr, nr, -1.0, None, ADD, None)
            tt(dv, t4, mag, si, MUL)
            are, aim = pc("a_re", 0, 16), pc("a_im", 0, 16)
            tt(dv, t0, are, are, MUL)
            tt(dv, t1, aim, aim, MUL)
            tt(dv, t0, t0, t1, ADD)
            recip(t0, t0)
            tt(dv, t1, nr, are, MUL)
            tt(dv, t2, t4, aim, MUL)
            tt(dv, t1, t1, t2, ADD)
            tt(dv, kr, t1, t0, MUL)
            tt(dv, t1, t4, are, MUL)
            tt(dv, t2, nr, aim, MUL)
            tt(dv, t1, t1, t2, SUB)
            tt(dv, ki, t1, t0, MUL)
            def b32(a):
                return a.unsqueeze(2).to_broadcast([P, 16, 32])
            c3 = lambda a: a.rearrange("p (q c) -> p q c", q=16)
            w1 = alloc(512)
            w2 = sq[:, 0, :]
            tt(dv, c3(w1), c3(cre), b32(kr), MUL, m_cl)
            tt(dv, c3(w2), c3(cim), b32(ki), MUL)
            tt(dv, w1, w1, w2, SUB)
            tt(dv, c3(w2), c3(cre), b32(ki), MUL)
            tt(dv, c3(cre), c3(cim), b32(kr), MUL)
            stt(cre, w2, -1.0, cre, MUL, SUB)
            lc1, lc2 = w1, cre
            memset(dv, ct[:, :, 0:1], 1.0)
            memset(dv, st[:, :, 0:1], 0.0)
            wc, ws = v(13), v(14)
            copy(dv, wc, co)
            copy(dv, ws, si)
            tmp = y[:, 0:8, :].rearrange("p a b -> p (a b)")
            n = 1
            while n < HT:
                bw = wc.unsqueeze(2).to_broadcast([P, 16, n])
                bs_ = ws.unsqueeze(2).to_broadcast([P, 16, n])
                ta = tmp[:, 0:16 * n].rearrange("p (q n) -> p q n", q=16)
                c0, s0 = ct[:, :, 0:n], st[:, :, 0:n]
                c1, s1 = ct[:, :, n:2 * n], st[:, :, n:2 * n]
                m0 = tt(dv, ta, s0, bs_, MUL)
                tt(dv, c1, c0, bw, MUL)
                tt(dv, c1, c1, ta, SUB)
                tt(dv, ta, s0, bw, MUL)
                tt(dv, s1, c0, bs_, MUL)
                tt(dv, s1, s1, ta, ADD)
                tt(dv, t0, wc, wc, MUL)
                tt(dv, t1, ws, ws, MUL)
                tt(dv, t2, wc, ws, MUL)
                tt(dv, wc, t0, t1, SUB)
                ts(dv, ws, t2, 2.0, None, MUL, None)
                n *= 2
            tab = dv.last()

            def keep_u(o, acc, d):
                return act(us[:, o, :], acc, ACT.Copy, d)

            linear(hs(), io["w_even"], 4, 8, keep_u, after=[hn], first=4)
            u_done = ac.last()

            wk = tiles(10)
            br, bi, p1, p2, p3, p4 = [wk[:, i, :] for i in range(6)]
            ysb = []
            prev = {"x": None, "pool": None, "dve": None}
            pe.wait(u_done, m_bl)
            yb = None
            for q in range(16):
                tl, j = q // 4, q % 4
                rows = slice(32 * j, 32 * j + 32)
                u_ = us[rows, tl, :]
                b1, a1 = bank()
                d1 = mm(a1, m_b[rows, tl * P:(tl + 1) * P], u_, True, True, mark=True)
                b2, a2 = bank()
                d2 = mm(a2, m_b2[rows, tl * P:(tl + 1) * P], u_, True, True, mark=True)
                m1 = act(br, a1, ACT.Copy, d1, prev["pool"], prev["dve"])
                m2 = act(bi, a2, ACT.Copy, d2)
                banks.free[b1], banks.free[b2] = m1, m2
                c_, s_ = [z[:, q, :].unsqueeze(1).to_broadcast([P, 2, HT]) for z in (ct, st)]
                po.wait(prev["x"], prev["dve"])
                dv.wait(prev["x"], prev["pool"])
                h2 = lambda a: a.rearrange("p (u t) -> p u t", u=2)
                tt(dv, h2(p1), h2(br), c_, MUL, m2, tab)
                tt(dv, h2(p2), h2(bi), s_, MUL)
                tt(dv, p1, p1, p2, ADD)
                tt(po, h2(p3), h2(bi), c_, MUL, m2, tab)
                tt(po, h2(p4), h2(br), s_, MUL)
                mz = tt(po, p3, p3, p4, SUB)
                decay = mag[:, q:q + 1].to_broadcast([P, HT])
                zr, zi = wk[:, 6, :], wk[:, 7, :]

                def scan(z, u, half, init, *after):
                    hs_ = slice(half * HT, half * HT + HT)
                    return dv.do(lambda e, decay=decay: e.tensor_tensor_scan(z[:, hs_], decay, u[:, hs_], init, MUL, ADD),
                                 *after)

                scan(zr, p1, 0, 0.0)
                scan(zi, p3, 0, 0.0, mz)
                er, ei = zr[:, HT - 1:HT], zi[:, HT - 1:HT]
                wq, vq = wc[:, q:q + 1], ws[:, q:q + 1]
                ts(dv, v(15)[:, 0:1], ei, vq, None, MUL, None)
                stt(v(15)[:, 1:2], er, wq, v(15)[:, 0:1], MUL, SUB)
                ts(dv, v(15)[:, 2:3], er, vq, None, MUL, None)
                stt(v(15)[:, 3:4], ei, wq, v(15)[:, 2:3], MUL, ADD)
                scan(zr, p1, 1, v(15)[:, 1:2])
                mzi = scan(zi, p3, 1, v(15)[:, 3:4])
                tt(dv, h2(p1), h2(zr), c_, MUL)
                tt(dv, h2(p2), h2(zi), s_, MUL)
                mxr = tt(dv, wk[:, 8, :], p1, p2, SUB)
                tt(po, h2(p3), h2(zr), s_, MUL, mzi)
                tt(po, h2(p4), h2(zi), c_, MUL)
                mxi = tt(po, wk[:, 9, :], p3, p4, ADD)
                if j == 0:
                    yb = bank()
                pe.wait(mxr, mxi)
                oc = slice(32 * q, 32 * q + 32)
                mm(yb[1][rows, :], lc1[:, oc], wk[:, 8, :], True, False)
                dy = mm(yb[1][rows, :], lc2[:, oc], wk[:, 9, :], False, True, mark=True)
                prev = {"x": dy, "pool": po.last(), "dve": dv.last()}
                if j == 3:
                    banks.free[yb[0]] = stt(us[:, tl, :], us[:, tl, :], pc("ssm_d", tl), yb[1], MUL, ADD, dy)
            yd = dv.last()

            sgm = wk[:, 0, :]

            def val(o, acc, d):
                return copy(dv, y[:, 4 + o, :], acc, d)

            def gate(o, acc, d):
                m = act(sgm, acc, ACT.Sigmoid, d, dv.last())
                tt(dv, y[:, 4 + o, :], y[:, 4 + o, :], sgm, MUL, m)
                return m

            linear([us[:, k, :] for k in range(4)], io["w_glu"], 4, 4, val, after=[yd])
            linear([us[:, k, :] for k in range(4)], io["w_glu"], 4, 4, gate, first=4)

            pw = wk[:, 9, :].rearrange("p (g d) -> p g d", g=4)
            m_pw = load(wk[:, 9, :], io["pool_w"])
            win = (2, 4, 8, 16)

            def pool(o, acc, d):
                a = [wk[:, 1, :], wk[:, 2, :]]
                u_ = wk[:, 3, :]
                m = act(u_, acc, ACT.Copy, d, dv.last())
                cur = u_
                dv.wait(m)
                sh = 1
                while sh < win[o]:
                    nxt = a[0] if cur is not a[0] else a[1]
                    tt(dv, nxt[:, sh:T], cur[:, sh:T], cur[:, 0:T - sh], ADD)
                    copy(dv, nxt[:, 0:sh], cur[:, 0:sh])
                    cur = nxt
                    sh *= 2
                w = win[o]
                oth = a[0] if cur is not a[0] else a[1]
                tt(dv, oth[:, 0:16], cur[:, 0:16], cc("invpos", 16 * o, 16), MUL)
                ts(dv, oth[:, 16:T], cur[:, 16:T], 1.0 / w, None, MUL, None)
                mp = tt(dv, wk[:, 4 + o % 2, :], oth, u_, SUB, (pe.last() if o >= 2 else None))
                b, a_ = bank()
                pe.wait(mp, m_pw)
                d2 = mm(a_, pw[:, o, :], wk[:, 4 + o % 2, :], True, True, mark=True)
                banks.free[b] = ts(dv, y[:, o, :], a_, pc("pool_scale", o), None, MUL, None, d2)
                return m

            linear(hs(), io["w_even"], 4, 8, pool, first=0)

            def zed(o, acc, d):
                sg = wk[:, 6 + o % 2, :]
                m = act(sg, acc, ACT.Silu, d, dv.last())
                tt(dv, y[:, o, :], y[:, o, :], sg, MUL, m)
                return m

            linear(hs(), io["w_even"], 8, 8, zed, first=8)
            linear([y[:, k, :] for k in range(8)], io["w_even_out"], 8, 8, residual, after=[dv.last()])
            barrier()

        def odd():
            top[0] = 0
            sq, rstd = tiles(2), alloc(T)
            sqs = [sq[:, 0, :], sq[:, 1, :]]
            hn = rmsnorm(x, h, lambda k: pc("odd_norm", k), 1e-6, sqs, rstd)
            PADW = T + 30
            g = alloc(2 * PADW).rearrange("p (k n) -> p k n", k=2)
            c = tiles(8)
            vb = tiles(2)
            pt = tiles(4)
            memset(po, g[:, :, 0:30], 0.0)
            pe.wait(hn)
            w = io["w_odd"]
            used = [None, None]
            for o in range(8):
                gb, gv = g[:, o % 2, :], g[:, o % 2, 30:PADW]

                def val(_, acc, d):
                    return act(vb[:, 0, :], acc, ACT.Copy, d, dv.last())

                def gate(_, acc, d):
                    m = act(vb[:, 1, :], acc, ACT.Sigmoid, d, dv.last())
                    tt(dv, gv, vb[:, 0, :], vb[:, 1, :], MUL, m, po.last())
                    return m

                linear(hs(), w, 1, 8, val, first=o)
                linear(hs(), w, 1, 8, gate, first=8 + o)
                mg = dv.last()
                cw = lambda k, o=o: pc("conv_w", 31 * o + k)
                ts(dv, c[:, o, :], gb[:, 0:T], cw(0), pc("conv_b", o), MUL, ADD)
                for k in range(1, 23):
                    stt(c[:, o, :], gb[:, k:k + T], cw(k), c[:, o, :], MUL, ADD)
                ts(po, pt[:, 0, :], gb[:, 23:23 + T], cw(23), None, MUL, None, mg)
                for k in range(24, 31):
                    ts(po, pt[:, 1, :], gb[:, k:k + T], cw(k), None, MUL, None)
                    mp = tt(po, pt[:, 0, :], pt[:, 0, :], pt[:, 1, :], ADD)
                md = tt(dv, c[:, o, :], c[:, o, :], pt[:, 0, :], ADD, mp)
                po.wait(md)
            b, acc = bank()
            pe.wait(dv.last())
            for k in range(8):
                d = mm(acc, ones, c[:, k, :], k == 0, k == 7, mark=(k == 7))
            mu_ = vb[:, 0, :]
            banks.free[b] = ts(dv, mu_, acc, 1.0 / 1024, None, MUL, None, d)
            b, acc = bank()
            r = []
            for k in range(8):
                m = tt(dv, c[:, k, :], c[:, k, :], mu_, SUB)
                m = act(sqs[k % 2], c[:, k, :], ACT.Square, m, r[k - 2] if k >= 2 else None)
                pe.wait(m)
                r.append(mm(acc, ones, sqs[k % 2], k == 0, k == 7, mark=True))
            m, banks.free[b] = rstd_of(acc, rstd, 1.0 / 1024, 1e-5, r[-1])
            dv.wait(m)
            for k in range(8):
                tt(dv, c[:, k, :], c[:, k, :], rstd, MUL)
                m = ts(dv, c[:, k, :], c[:, k, :], pc("ln_g", k), pc("ln_b", k), MUL, ADD)
                ml = act(c[:, k, :], c[:, k, :], ACT.Silu, m)

            def zed(o, acc, d):
                m = act(pt[:, o % 2, :], acc, ACT.Silu, d, dv.last(), po.last())
                tt(dv, c[:, o, :], c[:, o, :], pt[:, o % 2, :], MUL, m)
                return m

            linear(hs(), w, 8, 8, zed, first=16)
            linear([c[:, k, :] for k in range(8)], io["w_odd_out"], 8, 8, residual, after=[dv.last()])
            m = rmsnorm(x, x, lambda k: pc("final_norm", k), 1e-6, sqs, rstd, dv.last())
            barrier()

        def rope_into(dst, tmp, n, cos, sin):
            def f(o, acc, d):
                raw = tmp[:, 0, 0:n]
                m = act(raw, acc, ACT.Copy, d, pe.last(), dv.last())
                b, a = bank()
                pe.wait(m)
                d2 = mm(a[:, 0:n], cc("rot"), raw, True, True, mark=True)
                tt(dv, dst(o), raw, cos, MUL, m)
                banks.free[b] = tt(dv, tmp[:, 1, 0:n], a[:, 0:n], sin, MUL, d2)
                tt(dv, dst(o), dst(o), tmp[:, 1, 0:n], ADD)
                return m
            return f

        class Attn:

            def __init__(self):
                self.pr = Ring([alloc(T) for _ in range(4)])
                self.st = Ring([alloc(4) for _ in range(8)])
                self.pt = Ring([alloc(T) for _ in range(4)])

            def probs(self, q, k, nk, masks):
                b, acc = bank()
                d = mm(acc[:, 0:nk], q, k, True, True, mark=True)
                i, pr, f1 = self.pr.take()
                j, s4, f2 = self.st.take()
                for a, z, mask in masks:
                    tt(dv, acc[:, a:z], acc[:, a:z], mask, ADD, d)
                dv.do(lambda e, o=s4[:, 0:1], a=acc[:, 0:nk]: e.tensor_reduce(o, a, AX, MAX), f2)
                m = ts(dv, s4[:, 1:2], s4[:, 0:1], -0.125, None, MUL, None)
                m = ac.do(lambda e, o=pr[:, 0:nk], a=acc[:, 0:nk], s=s4: e.activation(
                    o, a, ACT.Exp, bias=s[:, 1:2], scale=0.125, accum_out=s[:, 2:3]), m, f1)
                banks.free[b] = m
                recip(s4[:, 3:4], s4[:, 2:3], m)
                self.m = m
                return (i, pr, j, s4)

            def transpose(self, pr, n, ready):
                b, a = bank()
                pe.wait(ready)
                nb = (n + P - 1) // P
                for t in range(nb):
                    w = min(P, n - t * P)
                    d = tr(a[0:w, t * P:(t + 1) * P], pr[:, t * P:t * P + w], mark=(t == nb - 1))
                i, pt, f = self.pt.take()
                rows = P if n >= P else n
                m = act(pt[0:rows, 0:nb * P], a[0:rows, 0:nb * P], ACT.Copy, d, f)
                banks.free[b] = m
                return i, pt, m, d

        def mixer_ab():
            top[0] = 0
            y = tiles(8)
            keep = top[0]
            sq, rstd = tiles(2), alloc(T)
            sqs = [sq[:, 0, :], sq[:, 1, :]]
            hn = rmsnorm(x, h, lambda k: pc("mix_norm", k), 1e-6, sqs, rstd)
            pe.wait(hn)
            w = io["w_ab"]
            q, k_ = tiles(4), tiles(4)
            vt = tiles(4)
            at = Attn()
            lam = alloc(8)
            lt = alloc(64)
            for i in range(2):
                tt(dv, lt, pc("lam", 128 * i, 64), pc("lam", 128 * i + 64, 64), MUL)
                m = dv.do(lambda e, o=lam[:, i:i + 1]: e.tensor_reduce(o, lt, AX, ADD))
            m = act(lam[:, 2:4], lam[:, 0:2], ACT.Exp, m)
            tt(dv, lam[:, 4:5], lam[:, 3:4], lam[:, 2:3], SUB, m)
            ts(dv, lam[:, 5:6], lam[:, 4:5], -LAM0, None, ADD, None)
            linear(hs(), w, 4, 8, rope_into(lambda o: q[:, o, :], sq, T, cc("cos"), cc("sin")), first=0)
            linear(hs(), w, 4, 8, rope_into(lambda o: k_[:, o, :], sq, T, cc("cos"), cc("sin")), first=4)
            linear_tok(hs(), io["w_av"], T, lambda t, a, d: act(vt[:, t, :], a, ACT.Copy, d))
            pe.wait(dv.last(), ac.last())
            for hd in range(4):
                ob = bank()
                for t in range(NT):
                    nk = (t + 1) * P
                    pr = []
                    for c in range(2):
                        r = slice(64 * c, 64 * c + 64)
                        pr.append(at.probs(q[r, hd, t * P:(t + 1) * P], k_[r, hd, 0:nk], nk,
                                           [(t * P, nk, cc("negmask"))]))
                    (i0, p0, j0, s0), (i1, p1, j1, s1) = pr
                    tt(dv, s1[:, 3:4], s1[:, 3:4], lam[:, 5:6], MUL)
                    m1 = ts(dv, p1[:, 0:nk], p1[:, 0:nk], s1[:, 3:4], None, MUL, None)
                    m = stt(p0[:, 0:nk], p0[:, 0:nk], s0[:, 3:4], p1[:, 0:nk], MUL, ADD)
                    at.pr.free[i1] = at.st.free[j0] = at.st.free[j1] = m
                    ip, pt, m, d = at.transpose(p0, nk, m)
                    at.pr.free[i0] = d
                    pe.wait(m)
                    for kt in range(t + 1):
                        d = mm(ob[1][:, t * P:(t + 1) * P], vt[:, kt, hd * P:(hd + 1) * P],
                               pt[:, kt * P:(kt + 1) * P], kt == 0, kt == t, mark=(kt == t))
                    at.pt.free[ip] = d
                m = act(sqs[0], ob[1], ACT.Square, d, pe.last())
                b, acc = bank()
                pe.wait(m)
                d = mm(acc, ones, sqs[0], True, True, mark=True)
                m, banks.free[b] = rstd_of(acc, rstd, 1.0 / 128, 1e-6, d)
                stt(y[:, hd, :], ob[1], pc("subln"), rstd, MUL, MUL, m)
                banks.free[ob[0]] = ts(dv, y[:, hd, :], y[:, hd, :], 1.0 - LAM0, None, MUL, None)
            barrier()

            top[0] = keep
            NC = 16
            rg = alloc(T)
            s1, s2, s3 = alloc(T), alloc(T), alloc(T)
            raw = alloc(2 * (T + 1)).rearrange("p (k n) -> p k n", k=2)
            AR = alloc(4 * 1024).rearrange("p (a t c s) -> p a t c s", a=4, t=NT, c=2)
            be, ka_, vf = tiles(4), tiles(4), tiles(4)
            PC = alloc(4 * NC).rearrange("p (a c) -> p a c", a=4)
            mark_wide = top[0]
            wa, gl = alloc(T), alloc(T)
            aa, sg_ = tiles(4), tiles(4)
            w2 = alloc(T)
            g2 = alloc(T)
            m_w2 = load(w2, io["w2a2"])
            m_g2 = load(g2, io["g2"])
            memset(po, raw[:, :, 0:1], 0.0)
            rk4 = lambda a: AR[:, a, :, 1, :]
            al4 = lambda a: AR[:, a, :, 0, :]
            v4 = lambda a: a.rearrange("p (t s) -> p t s", t=NT)
            c16 = lambda a: a.rearrange("p (c s) -> p c s", c=NC)

            def shift(dst):
                def f(o, acc, d):
                    r = raw[:, o % 2, :]
                    m = act(r[:, 1:T + 1], acc, ACT.Copy, d, dv.last(), po.last())
                    tt(dv, s1, r[:, 0:T], r[:, 1:T + 1], SUB, m)
                    out, ti = dst(o)
                    a, b_, c_ = s1, r[:, 1:T + 1], out
                    if len(out.shape) == 3:
                        a, b_ = v4(a), v4(b_)
                    stt(out, a, pc("mu", ti), b_, MUL, ADD)
                    return m
                return f

            linear(hs(), w, 4, 8, shift(lambda o: (rk4(o), o)), first=8)
            linear(hs(), w, 4, 8, shift(lambda o: (ka_[:, o, :], 4 + o)), first=12)
            linear(hs(), w, 4, 8, shift(lambda o: (vf[:, o, :], 8 + o)), first=16)
            linear(hs(), w, 2, 8, shift(lambda o: ((wa, gl)[o], 12 + o)), first=20)
            md = dv.last()
            m = act(wa[0:64, :], wa[0:64, :], ACT.Tanh, md)
            m = act(gl, gl, ACT.Sigmoid)
            pe.wait(m, md, m_w2, m_g2)
            for a in range(4):
                cols = slice(a * P, (a + 1) * P)
                b1, a1 = bank()
                d1 = mm(a1, w2[0:64, cols], wa[0:64, :], True, True, mark=True)
                m1 = act(sg_[:, a, :], a1, ACT.Sigmoid, d1, bias=pc("w0", a))
                banks.free[b1] = m1
                b2, a2 = bank()
                d2 = mm(a2, w2[64:128, cols], wa[64:128, :], True, True, mark=True)
                m2 = act(aa[:, a, :], a2, ACT.Sigmoid, d2, bias=pc("a0", a))
                banks.free[b2] = m2
                b3, a3 = bank()
                d3 = mm(a3, g2[:, cols], gl, True, True, mark=True)
                banks.free[b3] = act(y[:, 4 + a, :], a3, ACT.Copy, d3)
                r = rk4(a)
                kk = rg
                m = ts(dv, kk, ka_[:, a, :], pc("kk", a), None, MUL, None, m2, pe.last())
                m = act(s1, kk, ACT.Square, m, dv.last())
                b4, a4 = bank()
                pe.wait(m)
                d4 = mm(a4, bones, s1, True, True, mark=True)
                m, banks.free[b4] = rstd_of(a4, s1, 1.0, 1e-12, d4)
                tt(dv, kk, kk, s1, MUL, m)
                ts(dv, s1, aa[:, a, :], -1.0, pc("ka", a), ADD, MUL)
                ts(dv, s1, s1, 1.0, None, ADD, None)
                tt(dv, ka_[:, a, :], ka_[:, a, :], s1, MUL)
                stt(v4(s1), r, pc("rk", a), v4(ka_[:, a, :]), MUL, MUL)
                b5, a5 = bank()
                pe.wait(dv.last())
                d5 = mm(a5, bones, s1, True, True, mark=True)
                dv.do(lambda e, a=a: e.tensor_tensor_scan(s2, cc("scanm"), sg_[:, a, :], 0.0, MUL, ADD), m1)
                m = tt(dv, s3, s2, sg_[:, a, :], SUB)
                m = act(s3, s3, ACT.Exp, m, scale=-DECAY)
                m = act(sg_[:, a, :], s2, ACT.Exp, scale=DECAY)
                m = act(s2, s2, ACT.Exp, scale=-DECAY)
                copy(dv, PC[:, a, :], c16(s2)[:, :, 31], m)
                tt(dv, al4(a), v4(kk), v4(s3), MUL)
                tt(dv, r, r, v4(s2), MUL)
                tt(dv, kk, kk, aa[:, a, :], MUL)
                tt(dv, be[:, a, :], kk, sg_[:, a, :], MUL)
                tt(dv, ka_[:, a, :], ka_[:, a, :], sg_[:, a, :], MUL)
                banks.free[b5] = tt(dv, aa[:, a, :], a5, vf[:, a, :], MUL, d5)
            barrier()
            bonus = aa
            top[0] = mark_wide + 2 * T + 4 * T
            L = alloc(1024).rearrange("p (u t) -> p u t", u=32)
            M = alloc(1024).rearrange("p (s t) -> p s t", s=32)
            X = alloc(1024).rearrange("p (s t) -> p s t", s=32)
            tm = alloc(1024)
            for a in range(4):
                bks = [bank(), bank()]
                for t in range(NT):
                    for par in range(2):
                        r = slice(64 * par, 64 * par + 64)
                        d = mm(bks[par][1][:, t * P:(t + 1) * P], be[r, a, t * P:(t + 1) * P],
                               AR[r, a, t, 0, :], True, True, mark=True)
                for par in range(2):
                    acc = bks[par][1].rearrange("p (t s) -> p t s", t=NT)
                    for c in range(4):
                        pr_ = slice(32 * c, 32 * c + 32)
                        u0 = (2 * a + par) * 4
                        m = tt(dv, L[pr_, u0:u0 + 4, :], acc[pr_, :, 32 * c:32 * c + 32],
                               cc("nstrict", 32 * c, 32)[pr_, :].unsqueeze(1).to_broadcast([32, 4, 32]),
                               MUL, d)
                    banks.free[bks[par][0]] = m
            ml = dv.last()
            d1, d2 = scratch
            mdm = s_sh.start(po, d1.rearrange("c s u t -> (c s) u t"), L, ml)
            for c in range(4):
                mdm = s_sh.start(po, M[32 * c:32 * c + 32, :, :], d1[c].rearrange("s u t -> u s t"), mdm)
            dv.wait(mdm)
            copy(dv, X.rearrange("p s t -> p (s t)"), cc("eye32"))
            for s in range(30, -1, -1):
                n = 31 - s
                tmv = tm[:, 0:n * n].rearrange("p (t j) -> p t j", t=n)
                tt(dv, tmv, X[:, s + 1:32, s + 1:32].rearrange("p j t -> p t j"),
                   M[:, s, s + 1:32].unsqueeze(1).to_broadcast([P, n, n]), MUL)
                mx = dv.do(lambda e, s=s, tmv=tmv: e.tensor_reduce(X[:, s, s + 1:32], tmv, AX, ADD))
            mdm = s_sh.start(po, d2.rearrange("c u s t -> (c u) s t"), X, mx)
            for c in range(4):
                mdm = s_sh.start(po, L[32 * c:32 * c + 32, :, :], d2[c].rearrange("u s t -> s u t"), mdm)
            top[0] = top[0] - 3 * 1024
            G = h[:, :, :].rearrange("p k t -> p (k t)").rearrange("p (a c k) -> p a c k", a=4, c=NC)
            N = alloc(4 * 1024).rearrange("p (a c k) -> p a c k", a=4, c=NC)
            be_hat = s1
            ka_hat = s2
            scr = area[:, mark_wide:mark_wide + 1024]
            ML = Ring([alloc(384) for _ in range(2)])
            TE = Ring([alloc(P) for _ in range(2)])
            UW = Ring([alloc(P) for _ in range(2)])
            RH = scr[:, 0:256].rearrange("p (r c) -> p r c", r=2)
            VT = scr[:, 256:384]
            D_ = rg
            barrier()
            BX, KX = [raw[:, i, 0:T].rearrange("p (r c k) -> p r c k", r=2, c=4) for i in range(2)]
            dv.wait(mdm)
            for a in range(4):
                tt(dv, c16(be_hat), c16(be[:, a, :]), PC[:, a, :].unsqueeze(2).to_broadcast([P, NC, 32]), MUL,
                   pe.last())
                mh = tt(dv, c16(ka_hat), c16(ka_[:, a, :]), PC[:, a, :].unsqueeze(2).to_broadcast([P, NC, 32]),
                        MUL)
                pe.wait(mh)
                for t in range(NT):
                    b, acc = bank()
                    sl = slice(t * P, (t + 1) * P)
                    tr(acc[:, 0:128], AR[:, a, t, 0, :])
                    tr(acc[:, 128:256], vf[:, a, sl])
                    tr(acc[:, 256:384], be_hat[:, sl])
                    d = tr(acc[:, 384:512], ka_hat[:, sl], mark=True)
                    ac.wait(d)
                    dv.wait(d)
                    act(RH[:, :, 64:128], acc[:, 0:128].rearrange("p (r c) -> p r c", r=2), ACT.Copy)
                    mt = act(VT, acc[:, 128:256], ACT.Copy)

                    def spread(i):
                        return acc[:, i:i + 128].rearrange("p (r k) -> p r k", r=2).unsqueeze(2)\
                            .to_broadcast([P, 2, 4, 64])
                    def cmask(n):
                        return cc(n).unsqueeze(1).unsqueeze(3).to_broadcast([P, 2, 4, 64])
                    dv.wait(mt)
                    for rr in range(2):
                        def sp3(i, rr=rr):
                            return acc[:, i + 64 * rr:i + 64 * rr + 64].unsqueeze(1).to_broadcast([P, 4, 64])
                        def cm3(n):
                            return cc(n).unsqueeze(2).to_broadcast([P, 4, 64])
                        tt(dv, BX[:, rr, :, :], sp3(256), cm3("ncm"), MUL)
                        mb = tt(dv, KX[:, rr, :, :], sp3(384), cm3("cm"), MUL)
                    banks.free[b] = mb
                    for par in range(2):
                        r = slice(64 * par, 64 * par + 64)
                        u = (2 * a + par) * 4 + t
                        b, acc1 = bank()
                        mm(acc1[:, 0:256], ka_[r, a, sl], AR[r, a, t, :, :], True, True)
                        d = mm(acc1[:, 256:384], be[r, a, sl], AR[r, a, t, 1, :], True, True, mark=True)
                        i1, mlt, f1 = ML.take()
                        m = tt(dv, mlt, acc1[:, 0:384], cc("ml"), MUL, d, f1)
                        banks.free[b] = m
                        i2, te, f2 = TE.take()
                        mte = tt(dv, te.rearrange("p (c t) -> p c t", c=4),
                                 L[:, u, :].unsqueeze(1).to_broadcast([P, 4, 32]),
                                 cc("cm").unsqueeze(2).to_broadcast([P, 4, 32]), MUL, f2)
                        b, acc2 = bank()
                        pe.wait(m, mt)
                        vv = VT[:, r]
                        d = mm(acc2[:, 0:64], mlt[:, 0:128], vv, True, True, mark=True)
                        m = act(RH[:, par, 0:64], acc2[:, 0:64], ACT.Copy, d)
                        banks.free[b] = m
                        b, acc3 = bank()
                        pe.wait(m, mte)
                        d = mm(acc3[:, 0:128], te, RH[:, par, :], True, True, mark=True)
                        TE.free[i2] = d
                        i3, uw, f3 = UW.take()
                        m = act(uw, acc3[:, 0:128], ACT.Copy, d, f3)
                        banks.free[b] = m
                        pe.wait(m, mb)
                        b, acc4 = bank()
                        d = mm(acc4[r, 0:256], uw[:, 64:128], BX[:, par, :, :], True, True, mark=True)
                        m = tt(dv, D_[r, 0:256].rearrange("p (c k) -> p c k", c=4),
                               cc("ident64")[r, :].unsqueeze(1).to_broadcast([64, 4, 64]),
                               PC[r, a, 4 * t:4 * t + 4].unsqueeze(2).to_broadcast([64, 4, 64]), MUL)
                        banks.free[b] = tt(dv, G[r, a, 4 * t:4 * t + 4, :],
                                           acc4[r, 0:256].rearrange("p (c k) -> p c k", c=4),
                                           D_[r, 0:256].rearrange("p (c k) -> p c k", c=4), ADD, d)
                        b, acc5 = bank()
                        for c in range(4):
                            o_ = acc5[r, 64 * c:64 * c + 64]
                            mm(o_, BX[:, par, c, :], uw[:, 0:64], c == 0, False)
                            d = mm(o_, KX[:, par, c, :], vv, False, c == 3, mark=(c == 3))
                        banks.free[b] = act(N[r, a, 4 * t:4 * t + 4, :],
                                            acc5[r, 0:256].rearrange("p (c k) -> p c k", c=4), ACT.Copy, d)
                        b, acc6 = bank()
                        mm(acc6[r, 0:128], uw[:, 64:128], mlt[:, 256:384], True, True)
                        mm(acc6[r, 128:256], vv, mlt[:, 128:256], True, False)
                        d = mm(acc6[r, 128:256], uw[:, 0:64], mlt[:, 256:384], False, True, mark=True)
                        ML.free[i1] = UW.free[i3] = d
                        tt(dv, AR[r, a, t, 1, :], AR[r, a, t, 1, :], acc6[r, 0:128], ADD, d)
                        banks.free[b] = copy(dv, vf[r, a, sl], acc6[r, 128:256])
                    ac.wait(d)
                    dv.wait(d)
            barrier()
            St = Ring([be[:, 0, 0:256].rearrange("p (a v) -> p a v", a=4),
                       be[:, 1, 0:256].rearrange("p (a v) -> p a v", a=4)])
            yb = [bank() for _ in range(4)]
            S = N[:, :, 0, :]
            ready = last_i = None
            for c in range(1, NC):
                pe.wait(ready)
                t, cs = c // 4, 32 * (c % 4)
                if c < NC - 1:
                    b, acc = bank()
                    for a in range(4):
                        for par in range(2):
                            r = slice(64 * par, 64 * par + 64)
                            d = mm(acc[r, 64 * a:64 * a + 64], G[r, a, c, :], S[r, a, :], True, True,
                                   mark=(a == 3 and par == 1))
                for a in range(4):
                    for par in range(2):
                        r = slice(64 * par, 64 * par + 64)
                        dy = mm(yb[a][1][r, 32 * c:32 * c + 32], S[r, a, :],
                                AR[r, a, t, 1, cs:cs + 32], True, True, mark=(a == 3 and par == 1))
                if c < NC - 1:
                    i, S2, f = St.take()
                    ready = tt(dv, S2, acc[:, 0:256].rearrange("p (a v) -> p a v", a=4), N[:, :, c, :], ADD,
                               d, f)
                    banks.free[b] = ready
                    if last_i is not None:
                        St.free[last_i] = dy
                    last_i = i
                    S = S2
            for a in range(4):
                tt(dv, vf[:, a, 32:T], vf[:, a, 32:T], yb[a][1][:, 32:T], ADD, dy)
                banks.free[yb[a][0]] = dv.last()
            for a in range(4):
                b, acc = bank()
                pe.wait(dv.last())
                d = mm(acc, bones, vf[:, a, :], True, True, mark=True)
                ts(dv, s1, acc, 1.0 / 64, None, MUL, None, d)
                banks.free[b] = dv.last()
                m = tt(dv, vf[:, a, :], vf[:, a, :], s1, SUB)
                m = act(s2, vf[:, a, :], ACT.Square, m)
                b, acc = bank()
                pe.wait(m)
                d = mm(acc, bones, s2, True, True, mark=True)
                m, banks.free[b] = rstd_of(acc, s1, 1.0 / 64, 64e-5, d)
                tt(dv, vf[:, a, :], vf[:, a, :], s1, MUL, m)
                ts(dv, vf[:, a, :], vf[:, a, :], pc("lnw", a), pc("lnb", a), MUL, ADD)
                tt(dv, vf[:, a, :], vf[:, a, :], bonus[:, a, :], ADD)
                tt(dv, y[:, 4 + a, :], y[:, 4 + a, :], vf[:, a, :], MUL)
            linear([y[:, k, :] for k in range(8)], io["w_ab_out"], 8, 8, residual, after=[dv.last()])
            barrier()

        def mixer_cd():
            top[0] = 0
            y = tiles(8)
            keep = top[0]
            sq, rstd = tiles(2), alloc(T)
            sqs = [sq[:, 0, :], sq[:, 1, :]]
            hn = rmsnorm(x, h, lambda k: pc("mix_norm", 8 + k), 1e-6, sqs, rstd)
            pe.wait(hn)
            w = io["w_cd"]
            q = tiles(4)
            kk = tiles(2)
            vt = alloc(NT * 280).rearrange("p (t c) -> p t c", t=NT)
            KCX = alloc(16 * 63).rearrange("p (j n) -> p j n", j=16)
            VCX = alloc(16 * 63).rearrange("p (j n) -> p j n", j=16)
            hidn = alloc(4 * 62).rearrange("p (a n) -> p a n", a=4)
            kcm = alloc(31)
            vcm = alloc(128)
            w2 = alloc(4 * 64).rearrange("p (a n) -> p a n", a=4)
            pb = alloc(4)
            at = Attn()
            m_w2 = load(w2.rearrange("p a n -> p (a n)"), io["nsa_w2"])
            linear(hs(), w, 4, 8, rope_into(lambda o: q[:, o, :], sq, T, cc("cos"), cc("sin")), first=0)
            linear(hs(), w, 2, 8, rope_into(lambda o: kk[:, o, :], sq, T, cc("cos"), cc("sin")), first=4)

            copy(po, KCX[:, :, 62:63], pc("pe_k", 0, 16).unsqueeze(2))
            copy(po, VCX[:, :, 62:63], pc("pe_v", 0, 16).unsqueeze(2))

            def blocks(o, acc, d):
                z = (KCX, VCX)[o // 2]
                g = o % 2
                for half in range(2):
                    r = slice(64 * half, 64 * half + 64)
                    src = acc.rearrange("p (n s) -> p s n", s=16)
                    for lo in range(2):
                        m = copy(dv, z[r, 8 * lo:8 * lo + 8, 31 * g:31 * g + 31],
                                 src[r, half:16:2, lo:lo + 31], d)
                return m

            linear(hs(), w, 4, 8, blocks, first=6)
            linear_tok(hs(), io["w_cv"], 280, lambda t, a, d: act(vt[:, t, :], a, ACT.Copy, d))
            gt = alloc(NT * 24).rearrange("p (t c) -> p t c", t=NT)
            act(gt, vt[:, :, 256:280], ACT.Sigmoid)
            pe.wait(dv.last(), po.last())
            for kv in range(2):
                z = (KCX, VCX)[kv]
                hb = [bank(), bank()]
                for c in range(4):
                    s, ap, mark = wload(io["nsa_w1"][kv, c], 1024)
                    pe.wait(mark)
                    for j in range(4):
                        for o in range(2):
                            d = mm(hb[o][1][:, 0:63], ap[:, j * 256 + o * P:j * 256 + o * P + P],
                                   z[:, 4 * c + j, :], c == 0 and j == 0, c == 3 and j == 3,
                                   mark=(j == 3 and o == 1))
                    slots.free[s] = d
                for o in range(2):
                    i = 2 * kv + o
                    m = copy(dv, pb[:, i:i + 1], hb[o][1][:, 62:63], d)
                    m = act(hidn[:, i, :], hb[o][1][:, 0:62], ACT.Gelu_apprx_tanh, m, bias=pb[:, i:i + 1])
                    banks.free[hb[o][0]] = m
            pe.wait(m, m_w2)
            b, acc = bank()
            for g in range(2):
                for o in range(2):
                    d = mm(acc[64 * g:64 * g + 64, 0:31], w2[:, o, :], hidn[:, o, 31 * g:31 * g + 31],
                           o == 0, o == 1, mark=True)
            banks.free[b] = rope_into(lambda o: kcm, sq, 31, cc("ccos"), cc("csin"))(0, acc[:, 0:31], d)
            b, acc = bank()
            for g in range(2):
                for o in range(2):
                    d = mm(acc[0:31, 64 * g:64 * g + 64], hidn[:, 2 + o, 31 * g:31 * g + 31], w2[:, 2 + o, :],
                           o == 0, o == 1, mark=True)
            banks.free[b] = act(vcm[0:31, :], acc[0:31, 0:128], ACT.Copy, d)
            pe.wait(dv.last(), ac.last())

            for hd in range(4):
                ob = bank()
                for t in range(NT):
                    nk = (t + 1) * P
                    for g in range(2):
                        r = slice(64 * g, 64 * g + 64)
                        qt = q[r, hd, t * P:(t + 1) * P]
                        out = ob[1][r, t * P:(t + 1) * P]
                        head = 4 * g + hd
                        parts = [(kcm[r, :], 31, [(0, 31, cc("cmpmask", 31 * t, 31))], 0),
                                 (kk[r, 0, 0:nk], nk, [(t * P, nk, cc("negmask"))], 1),
                                 (kk[r, 1, 0:nk], nk, [(t * P, nk, cc("negmask"))], 2)]
                        tp = []
                        for keys, n, masks, br in parts:
                            i, pr, j, s4 = at.probs(qt, keys, n, masks)
                            tt(dv, s4[:, 3:4], s4[:, 3:4], gt[:, t, 3 * head + br:3 * head + br + 1], MUL)
                            if br == 0:
                                tt(dv, s4[:, 3:4], s4[:, 3:4], cc("cmprow", t, 1), MUL)
                            m = ts(dv, pr[:, 0:n], pr[:, 0:n], s4[:, 3:4], None, MUL, None)
                            at.st.free[j] = m
                            ip, pt, m, d = at.transpose(pr, n, m)
                            at.pr.free[i] = d
                            tp.append((ip, pt, m))
                        ip, pt, m = tp[0]
                        pe.wait(m)
                        d = mm(out, vcm[0:31, r], pt[0:31, 0:128], True, False, mark=True)
                        at.pt.free[ip] = d
                        for br in (1, 2):
                            ip, pt, m = tp[br]
                            pe.wait(m)
                            for kt in range(t + 1):
                                d = mm(out, vt[:, kt, 128 * (br - 1) + 64 * g:128 * (br - 1) + 64 * g + 64],
                                       pt[:, kt * P:(kt + 1) * P], False, br == 2 and kt == t,
                                       mark=(kt == t))
                            at.pt.free[ip] = d
                banks.free[ob[0]] = act(y[:, hd, :], ob[1], ACT.Copy, d)
            barrier()

            top[0] = keep
            sq, rstd = tiles(2), alloc(T)
            qk = tiles(4)
            vt = tiles(4)
            raw = alloc(2 * (T + 3)).rearrange("p (k n) -> p k n", k=2)
            s1, s2, s3 = alloc(T), alloc(T), alloc(T)
            og = tiles(4)
            rows = tiles(4)
            cT = alloc(16)
            memset(po, raw[:, :, 0:3], 0.0)

            def conv(o, acc, d):
                r = raw[:, o % 2, :]
                m = act(r[:, 3:T + 3], acc, ACT.Copy, d, dv.last(), po.last())
                ts(dv, s1, r[:, 0:T], pc("mconv_w", 4 * o), pc("mconv_b", o), MUL, ADD, m)
                for k in range(1, 4):
                    mc = stt(s1, r[:, k:k + T], pc("mconv_w", 4 * o + k), s1, MUL, ADD)
                act(qk[:, o, :], s1, ACT.Silu, mc)
                dv.wait(ac.last())
                return m

            linear(hs(), w, 4, 8, conv, first=10)
            for o in range(2):
                ts(dv, qk[:, o, :], qk[:, o, :], 0.125, None, MUL, None)
            linear(hs(), w, 4, 8, lambda o, a, d: act(og[:, o, :], a, ACT.Sigmoid, d), first=14)
            linear_tok(hs(), io["w_dv"], T, lambda t, a, d: act(vt[:, t, :], a, ACT.Copy, d))
            fi = {}

            def gates(o, acc, d):
                m = ts(dv, s1[0:36, :], acc[0:36, :], pc("gate_b")[0:36, :], None, ADD, None, d)
                return m

            linear(hs(), w, 1, 8, gates, first=18)
            R = lambda a: a[32:36, :]
            m = act(R(s2), R(s1), ACT.Abs, dv.last())
            m = act(R(s2), R(s2), ACT.Exp, scale=-1.0)
            m = act(R(s2), R(s2), ACT.Ln, bias=1.0)
            ts(dv, R(s3), R(s1), 0.0, None, MIN, None, m)
            tt(dv, R(s3), R(s3), R(s2), SUB)
            Fr = rows[:, 0, :]
            dv.do(lambda e: e.tensor_tensor_scan(R(Fr), R(cst[:, CC["ones"]:CC["ones"] + 1])
                                                 .to_broadcast([4, T]), R(s3), 0.0, MUL, ADD))
            mF = dv.last()
            b, acc = bank()
            pe.wait(mF)
            d = mm(acc[0:4, :], cst[32:36, CC["ident"] + 32:CC["ident"] + 36], Fr[32:36, :], True, True,
                   mark=True)
            F0, G0, C0 = rows[0:4, 1, :], rows[0:4, 2, :], rows[0:4, 3, :]
            banks.free[b] = copy(dv, F0, acc[0:4, :], d)
            tt(dv, C0, s1[0:4, :], F0, SUB)
            one = cst[0:4, CC["ones"]:CC["ones"] + 1].to_broadcast([4, T])
            dv.do(lambda e: e.tensor_tensor_scan(G0, one, C0, 0.0, MUL, MAX))
            tt(dv, F0, F0, G0, ADD)
            ts(dv, F0, F0, -1.0, 85.0, MUL, MIN)
            ts(dv, F0, F0, -85.0, None, MAX, None)
            m = ts(dv, G0, G0, -1.0, None, MUL, None)
            b, acc = bank()
            pe.wait(m)
            for t in range(NT):
                d = tr(acc[:, 4 * t:4 * t + 4], C0[:, t * P:(t + 1) * P], mark=True)
            banks.free[b] = copy(dv, cT, acc[:, 0:16], d)
            pe.wait(dv.last(), ac.last())
            for hd in range(4):
                r = slice(64 * (hd % 2), 64 * (hd % 2) + 64)
                sel = cst[0:4, CC["sel"] + 128 * hd:CC["sel"] + 128 * hd + 128]
                bG, aG = bank()
                dG = mm(aG, sel, G0, True, True, mark=True)
                bM, aM = bank()
                dM = mm(aM, sel, F0, True, True, mark=True)
                m = act(s3, aM, ACT.Exp, dM, dv.last())
                banks.free[bM] = m
                bn, an = bank()
                bd, ad = bank()
                for s in range(NT):
                    n0 = s * P
                    bs, as_ = bank()
                    d = mm(as_[:, n0:T], qk[r, 2 + hd // 2, n0:n0 + P], qk[r, hd // 2, n0:T], True, True,
                           mark=True)
                    e1 = (s1, s2)[s % 2]
                    m = ts(dv, e1[:, n0:T], aG[:, n0:T], cT[:, 4 * s + hd:4 * s + hd + 1], 0.0, ADD, MIN,
                           dG, pe.last(), d)
                    m = act(e1[:, n0:T], e1[:, n0:T], ACT.Exp, m)
                    tt(dv, e1[:, n0:n0 + P], e1[:, n0:n0 + P], cc("triu"), MUL, m)
                    m = tt(dv, e1[:, n0:T], e1[:, n0:T], as_[:, n0:T], MUL)
                    banks.free[bs] = m
                    pe.wait(m)
                    mm(an[:, n0:T], vt[:, s, hd * P:(hd + 1) * P], e1[:, n0:T], s == 0, s == 3)
                    d = mm(ad[:, n0:T], ones, e1[:, n0:T], s == 0, s == 3, mark=True)
                banks.free[bG] = dv.last()
                m = act(s1, ad, ACT.Abs, d, dv.last())
                banks.free[bd] = m
                tt(dv, s1, s1, s3, MAX, m)
                recip(s1, s1)
                m = tt(dv, s1, s1, an, MUL)
                banks.free[bn] = m
                m = act(s2, s1, ACT.Square, m)
                b, acc = bank()
                pe.wait(m)
                d = mm(acc, ones, s2, True, True, mark=True)
                m, banks.free[b] = rstd_of(acc, s2, 1.0 / 128, 1e-6, d)
                stt(s1, s1, pc("mnorm", hd), s2, MUL, MUL, m)
                tt(dv, y[:, 4 + hd, :], s1, og[:, hd, :], MUL)
            linear([y[:, k, :] for k in range(8)], io["w_cd_out"], 8, 8, residual, after=[dv.last()])
            barrier()

        steps = [
            even,
            odd,
            lambda: swiglu("ffa_norm", 0, io["ffa_gate"], io["ffa_up"], io["ffa_down"]),
            mixer_ab,
            lambda: swiglu("ffb_norm", 0, io["ffb_gate"], io["ffb_up"], io["ffb_down"]),
            lambda: swiglu("ffa_norm", 1, io["ffa_gate"], io["ffa_up"], io["ffa_down"]),
            mixer_cd,
            lambda: swiglu("ffb_norm", 1, io["ffb_gate"], io["ffb_up"], io["ffb_down"]),
        ]
        for f in steps:
            f()
        top[0] = 0
        sq, rstd = tiles(2), alloc(T)
        rmsnorm(x, x, lambda k: pc("final_norm_2", k), 1e-6, [sq[:, 0, :], sq[:, 1, :]], rstd, dv.last())
        barrier()
        m = dv.last()
        mo = s_out.start(sp, io["out"], x[:, :, :], m)
        sp.wait(mo)

        block = ctx.enter_context(nc.Block())
        block.sync(lambda e: sp.play(e))
        block.tensor(lambda e: pe.play(e))
        block.vector(lambda e: dv.play(e))
        block.scalar(lambda e: ac.play(e))
        block.gpsimd(lambda e: po.play(e))


def _constants():
    f = np.float32
    c = np.zeros((P, NCONST), f)

    def put(name, a):
        a = np.asarray(a, f)
        c[:a.shape[0], CC[name]:CC[name] + a.shape[1]] = a

    i = np.arange(P)
    put("ident", np.eye(P))
    put("ones", np.ones((P, P)))
    put("bones", (i[:, None] // 64 == i[None, :] // 64))
    R = np.zeros((P, P), f)
    for b in (0, 64):
        for d in range(32):
            R[b + d + 32, b + d] = -1
            R[b + d, b + d + 32] = 1
    put("rot", R)
    inv = (10000.0 ** (-np.arange(0, 64, 2, dtype=f) / 64)).astype(f)

    def tabs(pos):
        ang = pos.astype(f)[None, :] * np.tile(inv, 4)[:, None]
        return np.cos(ang), np.sin(ang)

    a, b = tabs(np.arange(T))
    put("cos", a)
    put("sin", b)
    ends = 16 * np.arange(31) + 31
    a, b = tabs(ends)
    put("ccos", a)
    put("csin", b)
    put("negmask", np.where(i[None, :] <= i[:, None], 0.0, NEG))
    t = np.arange(T).reshape(4, P)
    put("cmpmask", np.concatenate([np.where(ends[None, :] <= t[k][:, None], 0.0, NEG) for k in range(4)], 1))
    put("cmprow", (t.T >= 31))
    same = i[:, None] // 32 == i[None, :] // 32
    strict = same & (i[:, None] < i[None, :])
    incl = same & (i[:, None] <= i[None, :])
    put("ml", np.concatenate([strict * 1.0, incl * 1.0, incl * -1.0], 1))
    put("nstrict", strict * -1.0)
    cm = i[:, None] // 32 == np.arange(4)[None, :]
    put("cm", cm)
    put("ncm", cm * -1.0)
    put("scanm", np.tile((np.arange(T) % 32 != 0)[None, :], (P, 1)))
    put("triu", i[:, None] <= i[None, :])
    put("ident64", np.tile(np.eye(64), (2, 1)))
    put("eye32", np.tile(np.eye(32).reshape(1, -1), (P, 1)))
    sel = np.zeros((4, 512), f)
    for k in range(4):
        sel[k, 128 * k:128 * k + 128] = 1
    put("sel", sel)
    pos = np.arange(1, 17, dtype=f)
    put("invpos", np.tile(np.concatenate([1 / np.minimum(pos, f(w)) for w in (2, 4, 8, 16)])[None, :], (P, 1)))
    return c


def _w(a):
    k, m = a.shape
    return np.ascontiguousarray(a.reshape(k // P, P, m // P, P).transpose(2, 1, 0, 3)).reshape(m // P, P, k)


def _col(v):
    return np.ascontiguousarray(v.reshape(-1, P).T)


def _layout(i):
    f = np.float32
    prm = np.zeros((P, NCOL), f)

    def put(name, a):
        prm[:a.shape[0], COL[name]:COL[name] + a.shape[1]] = a

    for name, key in [("even_norm", "even_norm"), ("pool_scale", "pool_scale"), ("ssm_d", "ssm_d"),
                      ("odd_norm", "odd_norm"), ("conv_b", "conv_b"), ("ln_g", "conv_ln_g"),
                      ("ln_b", "conv_ln_b"), ("mu", "rwkv_mu_2"), ("w0", "rwkv_w0_2"), ("a0", "rwkv_a0_2"),
                      ("kk", "rwkv_kk_2"), ("ka", "rwkv_ka_2"), ("lnw", "rwkv_lnw_2"), ("lnb", "rwkv_lnb_2"),
                      ("subln", "diff_subln_2"), ("mconv_b", "mlstm_conv_b_2"), ("mnorm", "mlstm_norm_2")]:
        put(name, _col(i[key][0]))
    put("final_norm", _col(i["final_norm"]))
    put("final_norm_2", _col(i["final_norm_2"]))
    for n in ("ffa_norm", "mix_norm", "ffb_norm"):
        put(n, _col(i[n + "_2"].reshape(-1)))
    put("rk", _col(i["rwkv_rk_2"][0].reshape(-1)))
    put("log_dt", np.repeat(i["ssm_log_dt"][0].reshape(16, 2).T, 64, axis=0))
    put("a_re", i["ssm_a_re"][0].reshape(16, P).T)
    put("a_im", i["ssm_a_im"][0].reshape(16, P).T)
    put("conv_w", i["conv_w"][0].reshape(31, 8, P).transpose(2, 1, 0).reshape(P, 248))
    put("mconv_w", i["mlstm_conv_w_2"][0].reshape(4, 4, P).transpose(2, 1, 0).reshape(P, 16))
    gb = np.zeros((P, 1), f)
    gb[0:4, 0] = i["mlstm_ig_b_2"][0]
    gb[32:36, 0] = i["mlstm_fg_b_2"][0]
    put("gate_b", gb)
    put("lam", np.tile(i["diff_lam_2"][0].reshape(1, 256), (P, 1)))
    put("pe_k", i["nsa_pe_k_2"][0].reshape(16, P).T)
    put("pe_v", i["nsa_pe_v_2"][0].reshape(16, P).T)

    out = {"params": prm, "consts": _constants()}
    out["x"] = np.ascontiguousarray(i["x"][0].T.reshape(8, P, T).transpose(1, 0, 2))
    out["w_even"] = _w(i["even_w_in"][0])
    out["w_glu"] = _w(i["ssm_w_glu"][0])
    out["w_even_out"] = _w(i["even_w_out"][0])
    out["pool_w"] = np.ascontiguousarray(i["pool_w"][0].transpose(1, 0, 2)).reshape(P, 512)
    for n in ("re", "im"):
        b = i["ssm_b_" + n][0].reshape(4, 4, 2, 64, 16)
        z = np.zeros((4, 2, 16, 4, 2, 64), f)
        for g in range(2):
            z[:, g, :, :, g, :] = b[:, :, g].transpose(1, 3, 0, 2)
        out["b_" + n] = z.reshape(P, 512)
    cs = []
    for n in ("re", "im"):
        c = i["ssm_c_" + n][0].reshape(16, 2, 16, 64)
        z = np.zeros((2, 64, 16, 2, 16), f)
        for g in range(2):
            z[g, :, :, g, :] = c[:, g].transpose(2, 0, 1)
        cs.append(z.reshape(P, 512))
    out["c_bd"] = np.concatenate(cs, 1)
    out["w_odd"] = _w(i["odd_w_in"][0])
    out["w_odd_out"] = _w(i["odd_w_out"][0])
    for n in ("ffa", "ffb"):
        for m in ("gate", "up", "down"):
            out[f"{n}_{m}"] = np.stack([_w(a) for a in i[f"{n}_{m}_2"]])
    ab = i["ab_w_in_2"][0]
    out["w_ab"] = _w(np.concatenate([ab[:, :1024], ab[:, 1536:]], 1))
    out["w_av"] = np.ascontiguousarray(ab[:, 1024:1536]).reshape(8, P, 512)
    out["w_ab_out"] = _w(i["ab_w_out_2"][0])
    out["w2a2"] = np.concatenate([i["rwkv_w2_2"][0], i["rwkv_a2_2"][0]], 0)
    out["g2"] = np.ascontiguousarray(i["rwkv_g2_2"][0])
    cd = i["cd_w_in_2"][0]
    qc = cd[:, :512].reshape(1024, 2, 4, 64).transpose(0, 2, 1, 3).reshape(1024, 512)
    kc, vc, ks, vs, kw, vw = [cd[:, 512 + 128 * k:640 + 128 * k] for k in range(6)]
    cg = cd[:, 1280:1304]
    dq, dk, dv_ = cd[:, 1304:1560], cd[:, 1560:1816], cd[:, 1816:2328]
    di, df, dog = cd[:, 2328:2332], cd[:, 2332:2336], cd[:, 2336:2848]
    dup = [np.concatenate([z[:, 64 * g:64 * g + 64]] * 2, 1) for z in (kc, vc) for g in range(2)]
    ifg = np.zeros((1024, P), f)
    ifg[:, 0:4] = di
    ifg[:, 32:36] = df
    out["w_cd"] = _w(np.concatenate([qc, ks, kw] + dup + [dq, dk, dog, ifg], 1))
    out["w_cv"] = np.ascontiguousarray(np.concatenate([vs, vw, cg], 1)).reshape(8, P, 280)
    out["w_dv"] = np.ascontiguousarray(dv_).reshape(8, P, 512)
    w1 = np.stack([i["nsa_w1_k_2"][0], i["nsa_w1_v_2"][0]]).reshape(2, 4, 4, P, 256)
    out["nsa_w1"] = np.ascontiguousarray(w1.transpose(0, 1, 3, 2, 4)).reshape(2, 4, P, 1024)
    w2 = np.stack([i["nsa_w2_k_2"][0], i["nsa_w2_v_2"][0]]).reshape(4, P, 64)
    out["nsa_w2"] = np.ascontiguousarray(w2.transpose(1, 0, 2)).reshape(P, 256)
    wo = i["cd_w_out_2"][0]
    oc = wo[:512].reshape(2, 4, 64, 1024).transpose(1, 0, 2, 3).reshape(512, 1024)
    out["w_cd_out"] = _w(np.concatenate([oc, wo[512:]], 0))
    return {k: np.ascontiguousarray(v) for k, v in out.items()}


def kernel(**inputs):
    import concourse.bacc as _bacc
    from concourse.bass_utils import run_bass_kernel_spmd

    arrays = _layout({k: np.asarray(v) for k, v in inputs.items()})
    nc = _bacc.Bacc("TRN2", target_bir_lowering=False, num_devices=1)
    io = {k: nc.dram_tensor(f"in_{k}", a.shape, F32, kind="ExternalInput").ap() for k, a in arrays.items()}
    io["out"] = nc.dram_tensor("out_0", (P, 8, T), F32, kind="ExternalOutput").ap()
    build(nc, io)
    r = run_bass_kernel_spmd(nc, [{f"in_{k}": a for k, a in arrays.items()}], core_ids=[0])
    y = r.results[0]["out_0"]
    return np.ascontiguousarray(y.transpose(2, 1, 0).reshape(1, T, 1024))
```

```python
from contextlib import ExitStack
import math

import numpy as np

import concourse.bass as bass
from concourse import mybir

F32 = mybir.dt.float32
FR = mybir.dt.float32r
I32 = mybir.dt.int32
ACT = mybir.ActivationFunctionType
ALU = mybir.AluOpType
AX = mybir.AxisListType.X
MUL, ADD, SUB, MAX, MIN = ALU.mult, ALU.add, ALU.subtract, ALU.max, ALU.min

P = 128
T = 512
NT = T // P
SLOT = 1024
FF = 22
LAM0 = 0.8 - 0.6 * math.exp(-0.3 * 0)
DECAY = math.exp(-0.5)
NEG = -1e30

COLS = [
    ("even_norm", 8), ("pool_scale", 4), ("ssm_d", 4), ("log_dt", 16), ("a_re", 16), ("a_im", 16),
    ("odd_norm", 8), ("conv_w", 248), ("conv_b", 8), ("ln_g", 8), ("ln_b", 8), ("final_norm", 8),
    ("ffa_norm", 16), ("mix_norm", 16), ("ffb_norm", 16), ("mu", 14), ("w0", 4), ("a0", 4),
    ("kk", 4), ("ka", 4), ("rk", 4), ("lnw", 4), ("lnb", 4), ("subln", 1), ("mconv_w", 16),
    ("mconv_b", 4), ("gate_b", 1), ("mnorm", 4), ("final_norm_2", 8), ("lam", 256),
    ("pe_k", 16), ("pe_v", 16),
]
COL, NCOL = {}, 0
for _name, _n in COLS:
    COL[_name] = NCOL
    NCOL += _n

CONSTS = [
    ("ident", 128), ("ones", 128), ("bones", 128), ("rot", 128), ("cos", 512), ("sin", 512),
    ("ccos", 31), ("csin", 31), ("negmask", 128), ("cmpmask", 4 * 31), ("cmprow", 4),
    ("ml", 384), ("nstrict", 128), ("cm", 4), ("ncm", 4), ("scanm", 512), ("triu", 128),
    ("ident64", 64), ("eye32", 1024), ("sel", 512), ("invpos", 64),
]
CC, NCONST = {}, 0
for _name, _n in CONSTS:
    CC[_name] = NCONST
    NCONST += _n


class Lane:

    def __init__(self, sem, chained):
        self.sem, self.chained = sem, chained
        self.ops, self.n, self.seen = [], 0, {}

    def wait(self, *marks):
        for m in marks:
            if m is None:
                continue
            if isinstance(m, list):
                self.wait(*m)
                continue
            sem, value = m
            if self.seen.get(sem.name, 0) < value:
                self.seen[sem.name] = value
                self.ops.append(lambda e, s=sem, v=value: e.wait_ge(s, v))

    def do(self, fn, *after):
        if self.chained and self.n:
            self.wait((self.sem, self.n))
        self.wait(*after)
        self.n += 1
        self.ops.append(lambda e, s=self.sem: fn(e).then_inc(s, 1))
        return (self.sem, self.n)

    def plain(self, fn):
        self.ops.append(fn)

    def last(self):
        return (self.sem, self.n) if self.n else None

    def play(self, e):
        for op in self.ops:
            op(e)


class DmaSem:
    def __init__(self, sem):
        self.sem, self.n = sem, 0

    def start(self, lane, out, in_, *after):
        lane.wait(*after)
        self.n += 16
        lane.plain(lambda e, o=out, i=in_, s=self.sem: e.dma_start(o, i).then_inc(s, 16))
        return (self.sem, self.n)


class Free(dict):
    pass


class Ring:

    def __init__(self, bufs):
        self.bufs, self.free, self.at = bufs, Free((i, None) for i in range(len(bufs))), 0

    def take(self):
        while self.at % len(self.bufs) not in self.free:
            self.at += 1
        i = self.at % len(self.bufs)
        self.at += 1
        return i, self.bufs[i], self.free.pop(i)


def build(nc, io):
    ctx = ExitStack()
    with ctx:
        sems = {}

        def sem(n):
            if n not in sems:
                sems[n] = ctx.enter_context(nc.semaphore(n))
            return sems[n]

        prm = ctx.enter_context(nc.sbuf_tensor("prm", [P, NCOL], F32))
        cst = ctx.enter_context(nc.sbuf_tensor("cst", [P, NCONST], F32))
        base = (nc.sbuf_base + 31) // 32 * 32
        total = 53215 - NCOL - NCONST - 160
        mem = ctx.enter_context(nc.sbuf_tensor("mem", [P, total], F32))
        assert nc.sbuf_base == base + 4 * total
        parts = {}

        def memr(a, n):
            if (a, n) not in parts:
                parts[a, n] = nc.alloc_sbuf_tensor_at(f"part{a}_{n}", [P, n], FR, offset=base + 4 * a,
                                                      align_bytes=4)
            return parts[a, n]

        ps = ctx.enter_context(nc.psum_tensor("ps", [P, 8, 512], F32))
        scratch = [nc.dram_tensor(f"scratch{i}", (4, 32, 32, 32), F32, kind="Internal").ap() for i in range(2)]
        plan = []
        emit(nc, io, sem, (prm, cst, mem, memr, ps, scratch, total), plan, None)
        lanes = emit(nc, io, sem, (prm, cst, mem, memr, ps, scratch, total), [], plan)
        pe, dv, ac, po, sp = lanes
        block = ctx.enter_context(nc.Block())
        block.sync(lambda e: sp.play(e))
        block.tensor(lambda e: pe.play(e))
        block.vector(lambda e: dv.play(e))
        block.scalar(lambda e: ac.play(e))
        block.gpsimd(lambda e: po.play(e))


def emit(nc, io, sem, spaces, seen, plan):
    prm, cst, mem, memr, ps, scratch, total = spaces
    pe = Lane(sem("s_pe"), False)
    dv = Lane(sem("s_dve"), True)
    ac = Lane(sem("s_act"), True)
    po = Lane(sem("s_pool"), True)
    sp = Lane(sem("s_sp"), False)
    lanes = [pe, dv, ac, po]

    def split(a, n):
        r = memr(a, n)
        return r[:, :].bitcast(F32), r[:, :]

    class Pair:

        def __init__(self, hi, lo):
            self.hf, self.h = hi
            self.lf, self.l = lo
            self.ready = None

        def part(self, f):
            return Pair((f(self.hf), f(self.h)), (f(self.lf), f(self.l)))

    x = mem[:, 0:4096].rearrange("p (k t) -> p k t", k=8)
    hb, at_ = 4096, 4096 + 8192
    hmem = mem[:, hb:hb + 8192]

    def pairs(a, b, k, n=T):
        return [Pair(split(a + i * n, n), split(b + i * n, n)) for i in range(k)]

    h = pairs(hb, hb + 4096, 8)
    NR, NH = 2, 4
    raws = Ring([mem[:, at_ + i * SLOT:at_ + (i + 1) * SLOT] for i in range(NR)])
    at_ += NR * SLOT
    wts = Ring([Pair(split(at_ + 2 * i * SLOT, SLOT), split(at_ + (2 * i + 1) * SLOT, SLOT))
                for i in range(NH)])
    at_ += 2 * NH * SLOT
    nb = [mem[:, at_ + i * T:at_ + (i + 1) * T] for i in range(4)]
    sqs, ss, rstd = nb[0:2], nb[2], nb[3]
    at_ += 4 * T
    AREA = total - at_
    top = [0]

    def alloc(n):
        a = top[0]
        top[0] += n
        assert top[0] <= AREA, (top[0], AREA)
        return mem[:, at_ + a:at_ + a + n]

    def alloc_pairs(k, n=T):
        a = top[0]
        alloc(2 * k * n)
        return pairs(at_ + a, at_ + a + k * n, k, n)

    def tiles(k, n=T):
        return alloc(k * n).rearrange("p (k n) -> p k n", k=k)

    def pc(name, i=0, n=1):
        return prm[:, COL[name] + i:COL[name] + i + n]

    def cc(name, i=0, n=None):
        w = dict(CONSTS)[name] if n is None else n
        return cst[:, CC[name] + i:CC[name] + i + w]

    ident, ones, bones = cc("ident"), cc("ones"), cc("bones")
    banks = Ring([ps[:, i, :] for i in range(8)])
    wsem = [DmaSem(sem(f"s_w{i}")) for i in range(NR)]

    n_in = [0]

    def load(dst, src, *after):
        n_in[0] += 1
        return DmaSem(sem(f"s_in{n_in[0]}")).start(ac, dst, src, *after)

    s_sh = DmaSem(sem("s_sh"))
    s_out = DmaSem(sem("s_out"))
    s_c = DmaSem(sem("s_c"))

    def tt(ln, out, a, b, op, *after):
        return ln.do(lambda e: e.tensor_tensor(out, a, b, op), *after)

    def ts(ln, out, a, s1, s2, o0, o1, *after):
        if o1 is None:
            return ln.do(lambda e: e.tensor_scalar(out, a, s1, None, o0), *after)
        return ln.do(lambda e: e.tensor_scalar(out, a, s1, s2, o0, o1), *after)

    def stt(out, a, s, b, o0, o1, *after):
        return dv.do(lambda e: e.scalar_tensor_tensor(out=out, in0=a, scalar=s, in1=b, op0=o0, op1=o1),
                     *after)

    def copy(ln, out, a, *after):
        return ln.do(lambda e: e.tensor_copy(out, a), *after)

    def act(out, a, f, *after, **kw):
        return ac.do(lambda e: e.activation(out, a, f, **kw), *after)

    def recip(out, a, *after):
        return dv.do(lambda e: e.reciprocal(out, a), *after)

    def memset(ln, out, v, *after):
        return ln.do(lambda e: e.memset(out, v), *after)

    def mm(out, l, r, start, stop, mark=False):
        f = lambda e: e.matmul(out, l, r, start=start, stop=stop, skip_group_check=True)
        return pe.do(f) if mark else pe.plain(f)

    def tr(out, in_, mark=False):
        k = in_.shape[0]
        f = lambda e: e.transpose(out, in_, ident[0:k, 0:k])
        return pe.do(f) if mark else pe.plain(f)

    def barrier():
        marks = [l.last() for l in lanes]
        for l in lanes:
            l.wait(*marks)
        return marks

    def bank():
        i, ap, free = banks.take()
        pe.wait(free)
        return i, ap

    ready = []
    made = [0]
    AHEAD = 2

    def cut(dst, src, lane, *after):
        m = act(dst.h, src, ACT.Copy, *after)
        return m, tt(lane, dst.l, src, dst.hf, SUB, m, *after)

    def make(src, n, lane):
        i, raw, free = raws.take()
        r = raw[:, 0:n]
        dst = r.rearrange("p (a b) -> p a b", a=src.shape[1]) if len(src.shape) == 3 else r
        m = wsem[i].start(sp, dst, src, free)
        j, w, f = wts.take()
        w = w.part(lambda a: a[:, 0:n])
        _, m = cut(w, r, lane, m, f)
        raws.free[i] = m
        ready.append((j, w, m))

    def wload(src, n):
        lane = side[0]
        seen.append((src, n, lane is po))
        k = len(seen) - 1
        if plan is None:
            make(src, n, lane)
        else:
            while made[0] < min(k + 1 + AHEAD, len(plan)):
                s_, n_, p_ = plan[made[0]]
                make(s_, n_, po if p_ else dv)
                made[0] += 1
        return ready.pop(0)

    def mm3(out, l, r, start, stop, mark=False):
        mm(out, l.h, r.h, start, False)
        mm(out, l.h, r.l, False, False)
        return mm(out, l.l, r.h, False, stop, mark)

    m_c = s_c.start(ac, cst[:, :], io["consts"])
    m_p = load(prm[:, :], io["params"])
    m_xs = [DmaSem(sem(f"s_x{i}")).start(sp, x[:, 2 * i:2 * i + 2, :], io["x"][:, 2 * i:2 * i + 2, :])
            for i in range(4)]
    m_x = m_xs[-1]
    side = [dv]
    for l in lanes:
        l.wait(m_c, m_p)

    def linear_g(xs, w, n_out, kt, evac, after=(), first=0):
        pe.wait(*after)
        for o in range(n_out):
            b, acc = bank()
            for k0 in range(0, kt, 8):
                per = min(8, kt - k0)
                s, ap, mark = wload(w[first + o, :, k0 * P:(k0 + per) * P], per * P)
                pe.wait(mark)
                for j in range(per):
                    k = k0 + j
                    pe.wait(xs[k].ready)
                    done = mm3(acc, ap.part(lambda a: a[:, j * P:(j + 1) * P]), xs[k], k == 0, k == kt - 1,
                               mark=(j == per - 1))
                wts.free[s] = done
            banks.free[b] = evac(o, acc, done)
            yield

    def run(g):
        for _ in g:
            pass

    def weave(gens, width):
        gens, live = iter(gens), []
        while True:
            live = [g for g in live if next(g, live) is not live]
            g = next(gens, None) if len(live) < width else live
            if g is None:
                if not live:
                    return
            elif g is not live:
                if next(g, live) is not live:
                    live.append(g)

    def linear(*a, **kw):
        run(linear_g(*a, **kw))

    def linear_tok_g(xs, w, n, evac, after=(), halves=1):
        pe.wait(*after)
        for t0 in range(0, NT, NT // halves):
            ts_ = range(t0, t0 + NT // halves)
            bs = {t: bank() for t in ts_}
            for k0 in range(0, 8, 2):
                s, ap, mark = wload(w[k0:k0 + 2].rearrange("k p n -> p k n"), 2 * n)
                pe.wait(mark)
                for k in (k0, k0 + 1):
                    pe.wait(xs[k].ready)
                    for t in ts_:
                        xt = xs[k].part(lambda a: a[:, t * P:(t + 1) * P])
                        wk_ = ap.part(lambda a: a[:, (k - k0) * n:(k - k0 + 1) * n])
                        done = mm3(bs[t][1][:, 0:n], xt, wk_, k == 0, k == 7, mark=(t == ts_[-1]))
                wts.free[s] = done
            for t in ts_:
                banks.free[bs[t][0]] = evac(t, bs[t][1][:, 0:n], done)
            yield

    def linear_tok(*a, **kw):
        run(linear_tok_g(*a, **kw))

    def rstd_of(acc, out, scale, eps, done):
        m = ts(dv, out, acc, scale, eps, MUL, ADD, done)
        free = m
        m = recip(out, out)
        return act(out, out, ACT.Sqrt, m), free

    class Stat:

        def __init__(self):
            self.n, self.m = 0, None

        def add(self, ap, after):
            if self.n == 0:
                self.m = act(ss, ap, ACT.Square, after, pe.last())
            else:
                i = self.n % 2
                m = act(sqs[i], ap, ACT.Square, after, po.last())
                self.m = tt(po, ss, ss, sqs[i], ADD, m, self.m)
            self.n += 1
            return m if self.n > 1 else self.m

    def normed(stat, gain, eps, dst=None, scale=1.0 / 1024):
        b, acc = bank()
        pe.wait(stat.m)
        d = mm(acc, ones, ss, True, True, mark=True)
        m, banks.free[b] = rstd_of(acc, rstd, scale, eps, d)
        tmp = Ring(sqs)
        for k in range(8):
            if dst is None:
                stt(x[:, k, :], x[:, k, :], gain(k), rstd, MUL, MUL, m)
                continue
            i, t_, f = tmp.take()
            mr = stt(t_, x[:, k, :], gain(k), rstd, MUL, MUL, m, f)
            mh = act(dst[k].h, t_, ACT.Copy, mr)
            if k:
                tmp.free[j] = dst[k - 1].ready = tt(dv, dst[k - 1].l, prev, dst[k - 1].hf, SUB, mh1)
            j, prev, mh1 = i, t_, mh
        if dst is not None:
            dst[7].ready = tt(dv, dst[7].l, prev, dst[7].hf, SUB, mh1)
        return dv.last()

    def pair_up(srcs, dst, *after):
        m = [act(d.h, s_, ACT.Copy, *after) for s_, d in zip(srcs, dst)]
        for s_, d, m_ in zip(srcs, dst, m):
            d.ready = tt(dv, d.l, s_, d.hf, SUB, m_, *after)

    stat = Stat()
    for k in range(8):
        stat.add(x[:, k, :], m_xs[k // 2])
    for l in (dv, po):
        l.wait(*m_xs)
    cur = [stat]

    def residual_to(f):
        cur[0] = Stat()

        def g(o, acc, d):
            m = f(o, acc, d)
            cur[0].add(x[:, o, :], m)
            return m
        return g

    def swiglu(norm, i, wg, wu, wd):
        top[0] = 0
        hid = alloc_pairs(FF)
        m = normed(cur[0], lambda k: pc(norm, 8 * i + k), 1e-6, h)
        sg = Ring(sqs)
        ht = Ring([ss, rstd])
        for o in range(FF):
            for which, w in ((0, wg), (1, wu)):
                b, acc = bank()
                s, ap, mark = wload(w[i, o], 8 * P)
                pe.wait(mark)
                for k in range(8):
                    pe.wait(h[k].ready)
                    d = mm3(acc, ap.part(lambda a: a[:, k * P:(k + 1) * P]), h[k], k == 0, k == 7,
                            mark=(k == 7))
                wts.free[s] = d
                if which == 0:
                    j, sv, f = sg.take()
                    mg = act(sv, acc, ACT.Silu, d, f, m)
                    banks.free[b] = mg
                else:
                    j2, hv, f = ht.take()
                    mh = tt(dv, hv, acc, sv, MUL, d, mg, f)
                    sg.free[j] = banks.free[b] = mh
                    _, ht.free[j2] = cut(hid[o], hv, po, mh)
                    hid[o].ready = ht.free[j2]

        def add(o, acc, d):
            return stt(x[:, o, :], acc, 0.5, x[:, o, :], MUL, ADD, d)

        linear(hid, wd[i], 8, FF, residual_to(add))
        barrier()

    def residual(o, acc, d):
        return tt(dv, x[:, o, :], acc, x[:, o, :], ADD, d)

    def even():
        top[0] = 0
        y = tiles(8)
        us = tiles(4)
        HT = T // 2
        ct_at = top[0]
        ct = alloc(16 * HT).rearrange("p (q t) -> p q t", q=16)
        st = alloc(16 * HT).rearrange("p (q t) -> p q t", q=16)
        small = alloc(24 * 16)

        def v(i):
            return small[:, i * 16:(i + 1) * 16]

        m_b = alloc(512)
        cw = alloc(2 * 512)
        cre, cim = cw[:, 0:512], cw[:, 512:1024]
        m_cl = load(cw, io["c_bd"])
        m_bl = load(m_b, io["b_re"])
        m_b2 = alloc(512)
        m_bl = load(m_b2, io["b_im"])
        hn = normed(cur[0], lambda k: pc("even_norm", k), 1e-6, h)

        dt_, mag, co, si, kr, ki, t0, t1, t2, t3, t4, nr = [v(i) for i in range(12)]
        it = v(12).bitcast(I32)

        def exp_small(out, in_):
            ts(dv, t0, in_, 1.0 / math.log(2.0), None, MUL, None)
            ts(dv, t0, t0, -126.0, 126.0, MAX, MIN)
            ts(dv, t0, t0, 12582912.0, None, ADD, None)
            ts(dv, t0, t0, -12582912.0, None, ADD, None)
            stt(t1, t0, -0.693359375, in_, MUL, ADD)
            stt(t1, t0, 2.12194440e-4, t1, MUL, ADD)
            ts(dv, t1, t1, -0.7, 0.7, MAX, MIN)
            ts(dv, t2, t1, 1.0 / 5040, 1.0 / 720, MUL, ADD)
            for c in (1.0 / 120, 1.0 / 24, 1.0 / 6, 0.5, 1.0, 1.0):
                tt(dv, t2, t2, t1, MUL)
                ts(dv, t2, t2, c, None, ADD, None)
            ts(dv, it, t0, 127.0, 8388608.0, ADD, MUL)
            return tt(dv, out, t2, v(12), MUL)

        exp_small(dt_, pc("log_dt", 0, 16))
        tt(dv, t3, pc("a_re", 0, 16), dt_, MUL)
        exp_small(mag, t3)
        tt(dv, t3, pc("a_im", 0, 16), dt_, MUL)
        ts(dv, t0, t3, 1.0 / (2 * math.pi), 12582912.0, MUL, ADD)
        ts(dv, t0, t0, -12582912.0, None, ADD, None)
        stt(t3, t0, -6.28125, t3, MUL, ADD)
        stt(t3, t0, -(2 * math.pi - 6.28125), t3, MUL, ADD)
        m = ts(dv, t3, t3, 3.1415925, -3.1415925, MIN, MAX)
        act(si, t3, ACT.Sin, m)
        m = act(t4, t3, ACT.Abs)
        m = ts(dv, t4, t4, -1.0, math.pi / 2, MUL, ADD, m)
        m = act(co, t4, ACT.Sin, m)
        tt(dv, nr, mag, co, MUL, m)
        ts(dv, nr, nr, -1.0, None, ADD, None)
        tt(dv, t4, mag, si, MUL)
        are, aim = pc("a_re", 0, 16), pc("a_im", 0, 16)
        tt(dv, t0, are, are, MUL)
        tt(dv, t1, aim, aim, MUL)
        tt(dv, t0, t0, t1, ADD)
        recip(t0, t0)
        tt(dv, t1, nr, are, MUL)
        tt(dv, t2, t4, aim, MUL)
        tt(dv, t1, t1, t2, ADD)
        tt(dv, kr, t1, t0, MUL)
        tt(dv, t1, t4, are, MUL)
        tt(dv, t2, nr, aim, MUL)
        tt(dv, t1, t1, t2, SUB)
        tt(dv, ki, t1, t0, MUL)
        def b32(a):
            return a.unsqueeze(2).to_broadcast([P, 16, 32])
        c3 = lambda a: a.rearrange("p (q c) -> p q c", q=16)
        w1 = rstd
        w2 = sqs[0]
        dv.wait(ac.last())
        tt(dv, c3(w1), c3(cre), b32(kr), MUL, m_cl)
        tt(dv, c3(w2), c3(cim), b32(ki), MUL)
        tt(dv, w1, w1, w2, SUB)
        tt(dv, c3(w2), c3(cre), b32(ki), MUL)
        tt(dv, c3(cre), c3(cim), b32(kr), MUL)
        stt(cre, w2, -1.0, cre, MUL, SUB)
        lc1, lc2 = w1, cre
        def keep_u(o, acc, d):
            return act(us[:, o, :], acc, ACT.Copy, d)

        def zed(o, acc, d):
            return act(y[:, o, :], acc, ACT.Silu, d)

        side[0] = po
        linear(h, io["w_even"], 4, 8, keep_u, first=4)
        u_done = ac.last()
        linear(h, io["w_even"], 8, 8, zed, first=8)
        wk = tiles(12)

        memset(dv, ct[:, :, 0:1], 1.0)
        memset(dv, st[:, :, 0:1], 0.0)
        wc, ws = v(13), v(14)
        copy(dv, wc, co)
        copy(dv, ws, si)
        tmp = wk[:, 0:4, :].rearrange("p a b -> p (a b)")
        n = 1
        while n < HT:
            bw = wc.unsqueeze(2).to_broadcast([P, 16, n])
            bs_ = ws.unsqueeze(2).to_broadcast([P, 16, n])
            ta = tmp[:, 0:16 * n].rearrange("p (q n) -> p q n", q=16)
            c0, s0 = ct[:, :, 0:n], st[:, :, 0:n]
            c1, s1 = ct[:, :, n:2 * n], st[:, :, n:2 * n]
            m0 = tt(dv, ta, s0, bs_, MUL)
            tt(dv, c1, c0, bw, MUL)
            tt(dv, c1, c1, ta, SUB)
            tt(dv, ta, s0, bw, MUL)
            tt(dv, s1, c0, bs_, MUL)
            tt(dv, s1, s1, ta, ADD)
            tt(dv, t0, wc, wc, MUL)
            tt(dv, t1, ws, ws, MUL)
            tt(dv, t2, wc, ws, MUL)
            tt(dv, wc, t0, t1, SUB)
            ts(dv, ws, t2, 2.0, None, MUL, None)
            n *= 2
        tab = dv.last()

        h2 = lambda a: a.rearrange("p (u t) -> p u t", u=2)
        sets = Ring([wk[:, 0:6, :], wk[:, 6:12, :]])
        yb = {}
        pe.wait(u_done, m_bl)

        def s5(q):
            tl, j = q // 4, q % 4
            rows = slice(32 * j, 32 * j + 32)
            u_ = us[rows, tl, :]
            i, st6, free = sets.take()
            br, bi, p1, p2, p3, p4 = [st6[:, n, :] for n in range(6)]
            if j == 0:
                yb[tl] = bank()
            b1, a1 = bank()
            d1 = mm(a1, m_b[rows, tl * P:(tl + 1) * P], u_, True, True, mark=True)
            b2, a2 = bank()
            d2 = mm(a2, m_b2[rows, tl * P:(tl + 1) * P], u_, True, True, mark=True)
            banks.free[b1] = m1 = act(br, a1, ACT.Copy, d1, tab, free)
            banks.free[b2] = m2 = act(bi, a2, ACT.Copy, d2)
            c_, s_ = [z[:, q, :].unsqueeze(1).to_broadcast([P, 2, HT]) for z in (ct, st)]
            tt(po, h2(p3), h2(bi), c_, MUL, m2, tab)
            tt(po, h2(p4), h2(br), s_, MUL)
            mz = tt(po, p3, p3, p4, SUB)
            tt(dv, h2(p1), h2(br), c_, MUL, m2, tab)
            tt(dv, h2(p2), h2(bi), s_, MUL)
            tt(dv, p1, p1, p2, ADD)
            yield
            decay = mag[:, q:q + 1].to_broadcast([P, HT])

            def scan(z, half, init, *after):
                hs_ = slice(half * HT, half * HT + HT)
                return dv.do(lambda e: e.tensor_tensor_scan(z[:, hs_], decay, z[:, hs_], init, MUL, ADD),
                             *after)

            scan(p1, 0, 0.0)
            scan(p3, 0, 0.0, mz)
            er, ei = p1[:, HT - 1:HT], p3[:, HT - 1:HT]
            wq, vq = wc[:, q:q + 1], ws[:, q:q + 1]
            ts(dv, v(15)[:, 0:1], ei, vq, None, MUL, None)
            stt(v(15)[:, 1:2], er, wq, v(15)[:, 0:1], MUL, SUB)
            ts(dv, v(15)[:, 2:3], er, vq, None, MUL, None)
            stt(v(15)[:, 3:4], ei, wq, v(15)[:, 2:3], MUL, ADD)
            scan(p1, 1, v(15)[:, 1:2])
            mzi = scan(p3, 1, v(15)[:, 3:4])
            yield
            tt(dv, h2(br), h2(p1), c_, MUL)
            tt(dv, h2(bi), h2(p3), s_, MUL)
            mxr = tt(dv, br, br, bi, SUB)
            tt(po, h2(p2), h2(p1), s_, MUL, mzi)
            tt(po, h2(p4), h2(p3), c_, MUL)
            mxi = tt(po, p4, p2, p4, ADD)
            yield
            pe.wait(mxr, mxi)
            oc = slice(32 * q, 32 * q + 32)
            acc = yb[tl][1]
            mm(acc[rows, :], lc1[:, oc], br, True, False)
            dy = mm(acc[rows, :], lc2[:, oc], p4, False, True, mark=True)
            sets.free[i] = dy
            if j == 3:
                banks.free[yb[tl][0]] = stt(us[:, tl, :], us[:, tl, :], pc("ssm_d", tl), acc, MUL, ADD, dy)

        weave((s5(q) for q in range(16)), 2)
        yd = dv.last()

        sgm = wk[:, 0, :]

        def val(o, acc, d):
            return tt(dv, y[:, 4 + o, :], y[:, 4 + o, :], acc, MUL, d)

        def gate(o, acc, d):
            m = act(sgm, acc, ACT.Sigmoid, d, dv.last())
            tt(dv, y[:, 4 + o, :], y[:, 4 + o, :], sgm, MUL, m)
            return m

        us2 = pairs(at_ + ct_at, at_ + ct_at + 4 * T, 4)
        pair_up([us[:, k, :] for k in range(4)], us2, yd, po.last())
        linear(us2, io["w_glu"], 4, 4, val)
        linear(us2, io["w_glu"], 4, 4, gate, first=4)

        pw = wk[:, 9, :].rearrange("p (g d) -> p g d", g=4)
        m_pw = load(wk[:, 9, :], io["pool_w"])
        win = (2, 4, 8, 16)

        def pool(o, acc, d):
            a = [wk[:, 1, :], wk[:, 2, :]]
            u_ = wk[:, 3, :]
            m = act(u_, acc, ACT.Copy, d, dv.last())
            cur = u_
            dv.wait(m)
            sh = 1
            while sh < win[o]:
                nxt = a[0] if cur is not a[0] else a[1]
                tt(dv, nxt[:, sh:T], cur[:, sh:T], cur[:, 0:T - sh], ADD)
                copy(dv, nxt[:, 0:sh], cur[:, 0:sh])
                cur = nxt
                sh *= 2
            w = win[o]
            oth = a[0] if cur is not a[0] else a[1]
            tt(dv, oth[:, 0:16], cur[:, 0:16], cc("invpos", 16 * o, 16), MUL)
            ts(dv, oth[:, 16:T], cur[:, 16:T], 1.0 / w, None, MUL, None)
            mp = tt(dv, wk[:, 4 + o % 2, :], oth, u_, SUB, (pe.last() if o >= 2 else None))
            b, a_ = bank()
            pe.wait(mp, m_pw)
            d2 = mm(a_, pw[:, o, :], wk[:, 4 + o % 2, :], True, True, mark=True)
            banks.free[b] = stt(y[:, o, :], a_, pc("pool_scale", o), y[:, o, :], MUL, MUL, d2)
            return m

        linear(h, io["w_even"], 4, 8, pool, first=0)

        pair_up([y[:, k, :] for k in range(8)], h, dv.last(), pe.last())
        linear(h, io["w_even_out"], 8, 8, residual_to(residual))
        side[0] = dv
        barrier()

    def odd():
        top[0] = 0
        hn = normed(cur[0], lambda k: pc("odd_norm", k), 1e-6, h)
        PADW = T + 30
        g = alloc(2 * PADW).rearrange("p (k n) -> p k n", k=2)
        gs = Ring([g[:, 0, :], g[:, 1, :]])
        c = tiles(8)
        z = tiles(8)
        vbs = Ring([tiles(2), tiles(2)])
        sums = Ring([alloc(T), alloc(T)])
        prods = Ring([alloc(T) for _ in range(3)])
        pads = memset(po, g[:, :, 0:30], 0.0)
        w = io["w_odd"]
        NV = 17
        total_b, total_acc = bank()
        convs, summed = [], []

        def conv(o, gi, gb, mg):
            cw = lambda k: pc("conv_w", 31 * o + k)
            j, sm, f = sums.take()
            ts(dv, c[:, o, :], gb[:, 0:T], cw(0), pc("conv_b", o), MUL, ADD)
            for k in range(1, NV):
                mv = stt(c[:, o, :], gb[:, k:k + T], cw(k), c[:, o, :], MUL, ADD)
                if NV + k - 1 < 31:
                    kk_ = NV + k - 1
                    if k == 1:
                        mp = ma = act(sm, gb[:, kk_:kk_ + T], ACT.Copy, mg, f, scale=cw(kk_))
                    else:
                        i, pr, fp = prods.take()
                        ma = act(pr, gb[:, kk_:kk_ + T], ACT.Copy, mg, fp, scale=cw(kk_))
                        prods.free[i] = mp = tt(po, sm, sm, pr, ADD, ma, mp)
                if k % 6 == 5:
                    yield
            gs.free[gi] = [mv, ma]
            yield
            m = tt(dv, c[:, o, :], c[:, o, :], sm, ADD, mp)
            sums.free[j] = m
            summed.append(m)
            yield

        def total(o):
            pe.wait(summed[o])
            return mm(total_acc, ones, c[:, o, :], o == 0, o == 7, mark=True)

        def advance(n):
            for _ in range(n):
                if convs and next(convs[0], True):
                    convs.pop(0)

        for o in range(8):
            i, vb, f = vbs.take()
            gi, gb, fg = gs.take()
            gv = gb[:, 30:PADW]
            res = {}

            def val(_, acc, d):
                return act(vb[:, 0, :], acc, ACT.Copy, d, f)

            def gate(_, acc, d):
                m = act(vb[:, 1, :], acc, ACT.Sigmoid, d, f)
                res["m"] = tt(dv, gv, vb[:, 0, :], vb[:, 1, :], MUL, m, fg, pads)
                return m

            def zed(_, acc, d):
                return act(z[:, o, :], acc, ACT.Silu, d)

            linear(h, w, 1, 8, val, first=o)
            advance(1)
            linear(h, w, 1, 8, gate, first=8 + o)
            if o > 1:
                total(o - 2)
            vbs.free[i] = res["m"]
            advance(2)
            linear(h, w, 1, 8, zed, first=16 + o)
            advance(3)
            convs.append(conv(o, gi, gb, res["m"]))
            advance(1)
        while convs:
            advance(1)
        total(6)
        done = total(7)
        vb = vbs.bufs[0]
        mu_ = vb[:, 0, :]
        banks.free[total_b] = ts(dv, mu_, total_acc, 1.0 / 1024, None, MUL, None, done)
        b, acc = bank()
        r = []
        for k in range(8):
            m = tt(dv, c[:, k, :], c[:, k, :], mu_, SUB)
            m = act(sqs[k % 2], c[:, k, :], ACT.Square, m, r[k - 2] if k >= 2 else None)
            pe.wait(m)
            r.append(mm(acc, ones, sqs[k % 2], k == 0, k == 7, mark=True))
        m, banks.free[b] = rstd_of(acc, rstd, 1.0 / 1024, 1e-5, r[-1])
        dv.wait(m)
        silus = []
        for k in range(8):
            tt(dv, c[:, k, :], c[:, k, :], rstd, MUL)
            m = ts(dv, c[:, k, :], c[:, k, :], pc("ln_g", k), pc("ln_b", k), MUL, ADD)
            silus.append(act(c[:, k, :], c[:, k, :], ACT.Silu, m))
            if k:
                tt(dv, c[:, k - 1, :], c[:, k - 1, :], z[:, k - 1, :], MUL, silus[k - 1])
        tt(dv, c[:, 7, :], c[:, 7, :], z[:, 7, :], MUL, silus[7])
        pair_up([c[:, k, :] for k in range(8)], h, dv.last(), pe.last())
        linear(h, io["w_odd_out"], 8, 8, residual_to(residual))
        m = normed(cur[0], lambda k: pc("final_norm", k), 1e-6)
        cur[0] = Stat()
        for k in range(8):
            cur[0].add(x[:, k, :], m)
        barrier()

    def rope_into(dst, tmp, n, cos, sin):
        def f(o, acc, d):
            i, (raw, prod), free = tmp.take()
            raw, prod = raw[:, 0:n], prod[:, 0:n]
            m = act(raw, acc, ACT.Copy, d, free)
            b, a = bank()
            pe.wait(m)
            d2 = mm(a[:, 0:n], cc("rot"), raw, True, True, mark=True)
            tt(dv, dst(o), raw, cos, MUL, m)
            banks.free[b] = tt(dv, prod, a[:, 0:n], sin, MUL, d2)
            tmp.free[i] = tt(dv, dst(o), dst(o), prod, ADD)
            return m
        return f

    class Attn:

        def __init__(self):
            self.pr = Ring([alloc(T) for _ in range(8)])
            self.st = Ring([alloc(4) for _ in range(16)])
            self.pt = Ring([alloc(T) for _ in range(6)])

        def probs(self, q, k, nk, masks):
            b, acc = bank()
            d = mm(acc[:, 0:nk], q, k, True, True, mark=True)
            i, pr, f1 = self.pr.take()
            j, s4, f2 = self.st.take()
            for a, z, mask in masks:
                tt(dv, acc[:, a:z], acc[:, a:z], mask, ADD, d)
            dv.do(lambda e, o=s4[:, 0:1], a=acc[:, 0:nk]: e.tensor_reduce(o, a, AX, MAX), f2)
            m = ts(dv, s4[:, 1:2], s4[:, 0:1], -0.125, None, MUL, None)
            m = ac.do(lambda e, o=pr[:, 0:nk], a=acc[:, 0:nk], s=s4: e.activation(
                o, a, ACT.Exp, bias=s[:, 1:2], scale=0.125, accum_out=s[:, 2:3]), m, f1)
            banks.free[b] = m
            return i, pr, j, s4, m

        def transpose(self, pr, n, ready):
            b, a = bank()
            pe.wait(ready)
            nb = (n + P - 1) // P
            for t in range(nb):
                w = min(P, n - t * P)
                d = tr(a[0:w, t * P:(t + 1) * P], pr[:, t * P:t * P + w], mark=(t == nb - 1))
            i, pt, f = self.pt.take()
            rows = P if n >= P else n
            m = act(pt[0:rows, 0:nb * P], a[0:rows, 0:nb * P], ACT.Copy, d, f)
            banks.free[b] = m
            return i, pt, m, d

    def mixer_ab():
        top[0] = 0
        y = tiles(8)
        keep = top[0]
        hn = normed(cur[0], lambda k: pc("mix_norm", k), 1e-6, h)
        w = io["w_ab"]
        dv.wait(ac.last())
        ac.wait(dv.last())
        sq = Ring([(nb[0], nb[1]), (nb[2], nb[3])])
        q, k_ = tiles(4), tiles(4)
        vt = tiles(4)
        at = Attn()
        lam = alloc(8)
        lt = alloc(64)
        for i in range(2):
            tt(dv, lt, pc("lam", 128 * i, 64), pc("lam", 128 * i + 64, 64), MUL)
            m = dv.do(lambda e, o=lam[:, i:i + 1]: e.tensor_reduce(o, lt, AX, ADD))
        m = act(lam[:, 2:4], lam[:, 0:2], ACT.Exp, m)
        tt(dv, lam[:, 4:5], lam[:, 3:4], lam[:, 2:3], SUB, m)
        ts(dv, lam[:, 5:6], lam[:, 4:5], -LAM0, None, ADD, None)
        linear(h, w, 4, 8, rope_into(lambda o: q[:, o, :], sq, T, cc("cos"), cc("sin")), first=0)
        linear(h, w, 4, 8, rope_into(lambda o: k_[:, o, :], sq, T, cc("cos"), cc("sin")), first=4)
        linear_tok(h, io["w_av"], T, lambda t, a, d: act(vt[:, t, :], a, ACT.Copy, d))
        pe.wait(dv.last(), ac.last())
        heads = {}

        def unit(hd, t):
            if t == 0:
                heads[hd] = bank()
            ob = heads[hd]
            nk = (t + 1) * P
            pr = []
            for c in range(2):
                r = slice(64 * c, 64 * c + 64)
                pr.append(at.probs(q[r, hd, t * P:(t + 1) * P], k_[r, hd, 0:nk], nk,
                                   [(t * P, nk, cc("negmask"))]))
            yield
            (i0, p0, j0, s0, m0), (i1, p1, j1, s1, m1) = pr
            recip(s0[:, 3:4], s0[:, 2:3], m0)
            recip(s1[:, 3:4], s1[:, 2:3], m1)
            tt(dv, s1[:, 3:4], s1[:, 3:4], lam[:, 5:6], MUL)
            ts(dv, p1[:, 0:nk], p1[:, 0:nk], s1[:, 3:4], None, MUL, None)
            mp = stt(p0[:, 0:nk], p0[:, 0:nk], s0[:, 3:4], p1[:, 0:nk], MUL, ADD)
            at.pr.free[i1] = at.st.free[j0] = at.st.free[j1] = mp
            yield
            ip, pt, m, d = at.transpose(p0, nk, mp)
            at.pr.free[i0] = d
            yield
            pe.wait(m)
            for kt in range(t + 1):
                d = mm(ob[1][:, t * P:(t + 1) * P], vt[:, kt, hd * P:(hd + 1) * P],
                       pt[:, kt * P:(kt + 1) * P], kt == 0, kt == t, mark=(kt == t))
            at.pt.free[ip] = d
            if t < NT - 1:
                return
            m = act(sqs[0], ob[1], ACT.Square, d)
            yield
            b, acc = bank()
            pe.wait(m)
            d = mm(acc, ones, sqs[0], True, True, mark=True)
            m, banks.free[b] = rstd_of(acc, rstd, 1.0 / 128, 1e-6, d)
            yield
            stt(y[:, hd, :], ob[1], pc("subln"), rstd, MUL, MUL, m)
            banks.free[ob[0]] = ts(dv, y[:, hd, :], y[:, hd, :], 1.0 - LAM0, None, MUL, None)

        weave((unit(hd, t) for hd in range(4) for t in range(NT)), 4)
        barrier()

        top[0] = keep
        NC = 16
        rg, s1, s2, s3 = nb
        raw = alloc(2 * (T + 1)).rearrange("p (k n) -> p k n", k=2)
        AR = alloc(4 * 1024).rearrange("p (a t c s) -> p a t c s", a=4, t=NT, c=2)
        BK = alloc(4 * 1024).rearrange("p (a t c s) -> p a t c s", a=4, t=NT, c=2)
        be4 = lambda a: BK[:, a, :, 0, :]
        ka4 = lambda a: BK[:, a, :, 1, :]
        vf = tiles(4)
        PC = alloc(4 * NC).rearrange("p (a c) -> p a c", a=4)
        mark_wide = top[0]
        wa, gl = alloc(T), alloc(T)
        aa, sg_ = tiles(4), tiles(4)
        w2 = alloc(T)
        g2 = alloc(T)
        m_w2 = load(w2, io["w2a2"])
        m_g2 = load(g2, io["g2"])
        m = memset(po, raw[:, :, 0:1], 0.0)
        raws_ = Ring([raw[:, 0, :], raw[:, 1, :]])
        raws_.free[0] = raws_.free[1] = m
        rk4 = lambda a: AR[:, a, :, 1, :]
        al4 = lambda a: AR[:, a, :, 0, :]
        v4 = lambda a: a.rearrange("p (t s) -> p t s", t=NT)
        c16 = lambda a: a.rearrange("p (c s) -> p c s", c=NC)

        def shift(dst):
            def f(o, acc, d):
                i, r, free = raws_.take()
                m = act(r[:, 1:T + 1], acc, ACT.Copy, d, free)
                tt(dv, s1, r[:, 0:T], r[:, 1:T + 1], SUB, m)
                out, ti = dst(o)
                a, b_ = s1, r[:, 1:T + 1]
                if len(out.shape) == 3:
                    a, b_ = v4(a), v4(b_)
                raws_.free[i] = stt(out, a, pc("mu", ti), b_, MUL, ADD)
                return m
            return f

        linear(h, w, 4, 8, shift(lambda o: (rk4(o), o)), first=8)
        linear(h, w, 4, 8, shift(lambda o: (ka4(o), 4 + o)), first=12)
        linear(h, w, 4, 8, shift(lambda o: (vf[:, o, :], 8 + o)), first=16)
        linear(h, w, 2, 8, shift(lambda o: ((wa, gl)[o], 12 + o)), first=20)
        md = dv.last()
        m = act(wa[0:64, :], wa[0:64, :], ACT.Tanh, md)
        m = act(gl, gl, ACT.Sigmoid)
        pe.wait(m, md, m_w2, m_g2)
        sets = [nb] + [[hmem[:, 2048 * i + T * j:2048 * i + T * j + T] for j in range(4)] for i in range(3)]

        def prep(a):
            kk, s1, s2, s3 = sets[a]
            cols = slice(a * P, (a + 1) * P)
            b1, a1 = bank()
            d1 = mm(a1, w2[0:64, cols], wa[0:64, :], True, True, mark=True)
            m1 = act(sg_[:, a, :], a1, ACT.Sigmoid, d1, bias=pc("w0", a))
            banks.free[b1] = m1
            b2, a2 = bank()
            d2 = mm(a2, w2[64:128, cols], wa[64:128, :], True, True, mark=True)
            m2 = act(aa[:, a, :], a2, ACT.Sigmoid, d2, bias=pc("a0", a))
            banks.free[b2] = m2
            b3, a3 = bank()
            d3 = mm(a3, g2[:, cols], gl, True, True, mark=True)
            banks.free[b3] = act(y[:, 4 + a, :], a3, ACT.Copy, d3)
            r = rk4(a)
            m = ts(dv, v4(kk), ka4(a), pc("kk", a), None, MUL, None, m2)
            m = act(s1, kk, ACT.Square, m)
            m_s2 = dv.do(lambda e: e.tensor_tensor_scan(s2, cc("scanm"), sg_[:, a, :], 0.0, MUL, ADD), m1)
            m_s3 = tt(dv, s3, s2, sg_[:, a, :], SUB)
            yield
            b4, a4 = bank()
            pe.wait(m)
            d4 = mm(a4, bones, s1, True, True, mark=True)
            m, banks.free[b4] = rstd_of(a4, s1, 1.0, 1e-12, d4)
            act(s3, s3, ACT.Exp, m_s3, scale=-DECAY)
            act(sg_[:, a, :], s2, ACT.Exp, scale=DECAY)
            m_e = act(s2, s2, ACT.Exp, scale=-DECAY)
            yield
            tt(dv, kk, kk, s1, MUL, m)
            ts(dv, s1, aa[:, a, :], -1.0, pc("ka", a), ADD, MUL)
            ts(dv, s1, s1, 1.0, None, ADD, None)
            tt(dv, ka4(a), ka4(a), v4(s1), MUL)
            m = stt(v4(s1), r, pc("rk", a), ka4(a), MUL, MUL)
            yield
            b5, a5 = bank()
            pe.wait(m)
            d5 = mm(a5, bones, s1, True, True, mark=True)
            copy(dv, PC[:, a, :], c16(s2)[:, :, 31], m_e)
            tt(dv, al4(a), v4(kk), v4(s3), MUL)
            tt(dv, r, r, v4(s2), MUL)
            tt(dv, kk, kk, aa[:, a, :], MUL)
            tt(dv, be4(a), v4(kk), v4(sg_[:, a, :]), MUL)
            tt(dv, ka4(a), ka4(a), v4(sg_[:, a, :]), MUL)
            banks.free[b5] = tt(dv, aa[:, a, :], a5, vf[:, a, :], MUL, d5)

        weave((prep(a) for a in range(4)), 3)
        barrier()
        bonus = aa
        top[0] = mark_wide + 2 * T + 4 * T
        L = alloc(1024).rearrange("p (u t) -> p u t", u=32)
        M = alloc(1024).rearrange("p (s t) -> p s t", s=32)
        X = alloc(1024).rearrange("p (s t) -> p s t", s=32)
        tm = alloc(1024)
        for a in range(4):
            bks = [bank(), bank()]
            for t in range(NT):
                for par in range(2):
                    r = slice(64 * par, 64 * par + 64)
                    d = mm(bks[par][1][:, t * P:(t + 1) * P], BK[r, a, t, 0, :],
                           AR[r, a, t, 0, :], True, True, mark=True)
            for par in range(2):
                acc = bks[par][1].rearrange("p (t s) -> p t s", t=NT)
                for c in range(4):
                    pr_ = slice(32 * c, 32 * c + 32)
                    u0 = (2 * a + par) * 4
                    m = tt(dv, L[pr_, u0:u0 + 4, :], acc[pr_, :, 32 * c:32 * c + 32],
                           cc("nstrict", 32 * c, 32)[pr_, :].unsqueeze(1).to_broadcast([32, 4, 32]),
                           MUL, d)
                banks.free[bks[par][0]] = m
        ml = dv.last()
        d1, d2 = scratch
        mdm = s_sh.start(po, d1.rearrange("c s u t -> (c s) u t"), L, ml)
        written = mdm
        for c in range(4):
            mdm = s_sh.start(po, M[32 * c:32 * c + 32, :, :], d1[c].rearrange("s u t -> u s t"), written)
        pair_up([y[:, k, :] for k in range(4)], h[0:4])
        linear(h[0:4], io["w_ab_out"][:, :, 0:4 * P], 8, 4, residual)
        dv.wait(mdm)
        copy(dv, X.rearrange("p s t -> p (s t)"), cc("eye32"))
        for s in range(30, -1, -1):
            n = 31 - s
            tmv = tm[:, 0:n * n].rearrange("p (t j) -> p t j", t=n)
            tt(dv, tmv, X[:, s + 1:32, s + 1:32].rearrange("p j t -> p t j"),
               M[:, s, s + 1:32].unsqueeze(1).to_broadcast([P, n, n]), MUL)
            mx = dv.do(lambda e, s=s, tmv=tmv: e.tensor_reduce(X[:, s, s + 1:32], tmv, AX, ADD))
        mdm = s_sh.start(po, d2.rearrange("c u s t -> (c u) s t"), X, mx)
        written = mdm
        for c in range(4):
            mdm = s_sh.start(po, L[32 * c:32 * c + 32, :, :], d2[c].rearrange("u s t -> s u t"), written)
        top[0] = top[0] - 3 * 1024
        G = hmem[:, 0:4096].rearrange("p (a c k) -> p a c k", a=4, c=NC)
        N = BK.rearrange("p a t c s -> p (a t c s)").rearrange("p (a c k) -> p a c k", a=4, c=NC)
        wa_gl = mem[:, at_ + mark_wide:at_ + mark_wide + 1024]
        spare = mem[:, at_ + top[0]:at_ + top[0] + 3 * 1024]
        high = hmem[:, 4096:8192]
        mains = [high[:, 0:1664], high[:, 1664:3328], spare[:, 0:1664]]
        diags = [high[:, 3328 + 256 * i:3584 + 256 * i] for i in range(3)]
        wides = [(wa_gl[:, 0:512], wa_gl[:, 512:1024]), (spare[:, 1664:2176], spare[:, 2176:2688]),
                 (raw[:, 0, 0:T], raw[:, 1, 0:T])]
        hats = [s1[:, 0:256], s1[:, 256:512], s2[:, 0:256]]
        sets = Ring(list(zip(mains, diags, wides, hats)))
        barrier()
        for l in lanes:
            l.wait(mdm)

        def unit(a, t):
            si, (main, D_, wide, hat), free = sets.take()
            RH = main[:, 0:256].rearrange("p (r c) -> p r c", r=2)
            VT, ml, te, uw = main[:, 256:384], main[:, 384:1152], main[:, 1152:1408], main[:, 1408:1664]
            BX, KX = [z.rearrange("p (r c k) -> p r c k", r=2, c=4) for z in wide]
            sl = slice(t * P, (t + 1) * P)
            pcs = PC[:, a, 4 * t:4 * t + 4]
            dv.wait(free)
            ac.wait(free)
            for i in range(2):
                mh = tt(dv, hat[:, i * P:(i + 1) * P].rearrange("p (c s) -> p c s", c=4),
                        BK[:, a, t, i, :].rearrange("p (c s) -> p c s", c=4),
                        pcs.unsqueeze(2).to_broadcast([P, 4, 32]), MUL)
            yield
            b, acc = bank()
            tr(acc[:, 0:128], AR[:, a, t, 0, :])
            d = tr(acc[:, 128:256], vf[:, a, sl], mark=True)
            pe.wait(mh)
            tr(acc[:, 256:384], hat[:, 0:128])
            dh = tr(acc[:, 384:512], hat[:, 128:256], mark=True)
            for par in range(2):
                r = slice(64 * par, 64 * par + 64)
                b1, acc1 = bank()
                mm(acc1[:, 0:256], BK[r, a, t, 1, :], AR[r, a, t, :, :], True, True)
                d1 = mm(acc1[:, 256:384], BK[r, a, t, 0, :], AR[r, a, t, 1, :], True, True, mark=True)
                mml = tt(dv, ml[:, 384 * par:384 * par + 384], acc1[:, 0:384], cc("ml"), MUL, d1)
                banks.free[b1] = mml
            act(RH[:, :, 64:128], acc[:, 0:128].rearrange("p (r c) -> p r c", r=2), ACT.Copy, dh)
            mt = act(VT, acc[:, 128:256], ACT.Copy)
            for par in range(2):
                u = (2 * a + par) * 4 + t
                mte = tt(dv, te[:, P * par:P * par + P].rearrange("p (c t) -> p c t", c=4),
                         L[:, u, :].unsqueeze(1).to_broadcast([P, 4, 32]),
                         cc("cm").unsqueeze(2).to_broadcast([P, 4, 32]), MUL)
            for out, i, mask in ((BX, 256, "ncm"), (KX, 384, "cm")):
                for par in range(2):
                    mb = tt(dv, out[:, par, :, :],
                            acc[:, i + 64 * par:i + 64 * par + 64].unsqueeze(1).to_broadcast([P, 4, 64]),
                            cc(mask).unsqueeze(2).to_broadcast([P, 4, 64]), MUL, dh, mt)
            banks.free[b] = mb
            yield
            b, acc = bank()
            pe.wait(mml, mt)
            for par in range(2):
                d = mm(acc[:, 64 * par:64 * par + 64], ml[:, 384 * par:384 * par + 128],
                       VT[:, 64 * par:64 * par + 64], True, True, mark=True)
            m = act(RH[:, :, 0:64], acc[:, 0:128].rearrange("p (r c) -> p r c", r=2), ACT.Copy, d)
            banks.free[b] = m
            yield
            b, acc = bank()
            pe.wait(m, mte)
            for par in range(2):
                d = mm(acc[:, P * par:P * par + P], te[:, P * par:P * par + P], RH[:, par, :], True, True,
                       mark=True)
            m = act(uw, acc[:, 0:256], ACT.Copy, d)
            banks.free[b] = m
            yield
            pe.wait(m, mb)
            b4, acc4 = bank()
            b5, acc5 = bank()
            b6, acc6 = bank()
            for par in range(2):
                r = slice(64 * par, 64 * par + 64)
                u_, w_ = uw[:, P * par:P * par + 64], uw[:, P * par + 64:P * par + P]
                mq = ml[:, 384 * par:384 * par + 384]
                d4 = mm(acc4[r, 0:256], w_, BX[:, par, :, :], True, True, mark=True)
                for c in range(4):
                    o_ = acc5[r, 64 * c:64 * c + 64]
                    mm(o_, BX[:, par, c, :], u_, True, False)
                    d5 = mm(o_, KX[:, par, c, :], VT[:, r], False, True, mark=(c == 3))
                mm(acc6[r, 0:128], w_, mq[:, 256:384], True, True)
                mm(acc6[r, 128:256], VT[:, r], mq[:, 128:256], True, False)
                d6 = mm(acc6[r, 128:256], u_, mq[:, 256:384], False, True, mark=True)
            D3 = D_.rearrange("p (c k) -> p c k", c=4)
            tt(dv, D3, cc("ident64").unsqueeze(1).to_broadcast([P, 4, 64]),
               pcs.unsqueeze(2).to_broadcast([P, 4, 64]), MUL)
            banks.free[b4] = tt(dv, G[:, a, 4 * t:4 * t + 4, :],
                                acc4[:, 0:256].rearrange("p (c k) -> p c k", c=4), D3, ADD, d4)
            m5 = act(N[:, a, 4 * t:4 * t + 4, :], acc5[:, 0:256].rearrange("p (c k) -> p c k", c=4),
                     ACT.Copy, d5)
            banks.free[b5] = m5
            tt(dv, AR[:, a, t, 1, :], AR[:, a, t, 1, :], acc6[:, 0:128], ADD, d6)
            m6 = copy(dv, vf[:, a, sl], acc6[:, 128:256])
            banks.free[b6] = m6
            sets.free[si] = [m5, m6, d6]

        weave((unit(a, t) for a in range(4) for t in range(NT)), 3)
        barrier()
        St = Ring([hmem[:, 4096 + 256 * i:4352 + 256 * i].rearrange("p (a v) -> p a v", a=4)
                   for i in range(2)])
        yb = [bank() for _ in range(4)]
        S = N[:, :, 0, :]
        ready = last_i = None
        for c in range(1, NC):
            pe.wait(ready)
            t, cs = c // 4, 32 * (c % 4)
            if c < NC - 1:
                b, acc = bank()
                for a in range(4):
                    for par in range(2):
                        r = slice(64 * par, 64 * par + 64)
                        d = mm(acc[r, 64 * a:64 * a + 64], G[r, a, c, :], S[r, a, :], True, True,
                               mark=(a == 3 and par == 1))
            for a in range(4):
                for par in range(2):
                    r = slice(64 * par, 64 * par + 64)
                    dy = mm(yb[a][1][r, 32 * c:32 * c + 32], S[r, a, :],
                            AR[r, a, t, 1, cs:cs + 32], True, True, mark=(a == 3 and par == 1))
            if c < NC - 1:
                i, S2, f = St.take()
                ready = tt(dv, S2, acc[:, 0:256].rearrange("p (a v) -> p a v", a=4), N[:, :, c, :], ADD,
                           d, f)
                banks.free[b] = ready
                if last_i is not None:
                    St.free[last_i] = dy
                last_i = i
                S = S2
        for a in range(4):
            tt(dv, vf[:, a, 32:T], vf[:, a, 32:T], yb[a][1][:, 32:T], ADD, dy)
            banks.free[yb[a][0]] = dv.last()
        sets = [(s1, s2)] + [(hmem[:, 5120 + 1024 * i:5632 + 1024 * i], hmem[:, 5632 + 1024 * i:6144 + 1024 * i])
                             for i in range(3)]
        summed = dv.last()

        def group(a):
            s1, s2 = sets[a]
            va = vf[:, a, :]
            b, acc = bank()
            pe.wait(summed)
            d = mm(acc, bones, va, True, True, mark=True)
            banks.free[b] = ts(dv, s1, acc, 1.0 / 64, None, MUL, None, d)
            m = tt(dv, va, va, s1, SUB)
            m = act(s2, va, ACT.Square, m)
            yield
            b, acc = bank()
            pe.wait(m)
            d = mm(acc, bones, s2, True, True, mark=True)
            m, banks.free[b] = rstd_of(acc, s1, 1.0 / 64, 64e-5, d)
            yield
            tt(dv, va, va, s1, MUL, m)
            ts(dv, va, va, pc("lnw", a), pc("lnb", a), MUL, ADD)
            tt(dv, va, va, bonus[:, a, :], ADD)
            tt(dv, y[:, 4 + a, :], y[:, 4 + a, :], va, MUL)

        weave((group(a) for a in range(4)), 3)
        pair_up([y[:, k, :] for k in range(4, 8)], h[4:8], dv.last(), ac.last(), pe.last())
        linear(h[4:8], io["w_ab_out"][:, :, 4 * P:8 * P], 8, 4, residual_to(residual))
        barrier()

    def mixer_cd():
        top[0] = 0
        y = tiles(8)
        keep = top[0]
        hn = normed(cur[0], lambda k: pc("mix_norm", 8 + k), 1e-6, h)
        dv.wait(ac.last())
        ac.wait(dv.last())
        sq = Ring([(nb[0], nb[1]), (nb[2], nb[3])])
        w = io["w_cd"]
        q = tiles(4)
        kk = tiles(2)
        vt = alloc(NT * 280).rearrange("p (t c) -> p t c", t=NT)
        KCX = alloc(1024).rearrange("p (j n) -> p j n", j=16)
        VCX = alloc(1024).rearrange("p (j n) -> p j n", j=16)
        CX = alloc_pairs(2, 1024)
        hidn = alloc(4 * 62).rearrange("p (a n) -> p a n", a=4)
        kcm = alloc(31)
        vcm = alloc(128)
        w2 = alloc(4 * 64).rearrange("p (a n) -> p a n", a=4)
        pb = alloc(4)
        at = Attn()
        m_w2 = load(w2.rearrange("p a n -> p (a n)"), io["nsa_w2"])

        copy(po, KCX[:, :, 62:63], pc("pe_k", 0, 16).unsqueeze(2))
        copy(po, VCX[:, :, 62:63], pc("pe_v", 0, 16).unsqueeze(2))
        memset(po, KCX[:, :, 63:64], 0.0)
        memset(po, VCX[:, :, 63:64], 0.0)

        def blocks(o, acc, d):
            z = (KCX, VCX)[o // 2]
            g = o % 2
            for half in range(2):
                r = slice(64 * half, 64 * half + 64)
                src = acc.rearrange("p (n s) -> p s n", s=16)
                for lo in range(2):
                    m = copy(dv, z[r, 8 * lo:8 * lo + 8, 31 * g:31 * g + 31],
                             src[r, half:16:2, lo:lo + 31], d)
            return m

        linear(h, w, 4, 8, blocks, first=6)
        cut(CX[0], KCX.rearrange("p j n -> p (j n)"), dv, dv.last(), po.last())
        cut(CX[1], VCX.rearrange("p j n -> p (j n)"), dv)
        cxm = dv.last()

        def compress():
            pe.wait(cxm)
            for kv in range(2):
                acc2 = [bank(), bank()]
                for c in range(4):
                    s, ap, mark = wload(io["nsa_w1"][kv, c], 1024)
                    pe.wait(mark)
                    for j in range(4):
                        for o in range(2):
                            d = mm3(acc2[o][1][:, 0:64],
                                    ap.part(lambda a: a[:, j * 256 + o * P:j * 256 + o * P + P]),
                                    CX[kv].part(lambda a: a[:, 64 * (4 * c + j):64 * (4 * c + j) + 64]),
                                    c == 0 and j == 0, c == 3 and j == 3, mark=(j == 3 and o == 1))
                    wts.free[s] = d
                    yield
                for o in range(2):
                    i = 2 * kv + o
                    m = copy(dv, pb[:, i:i + 1], acc2[o][1][:, 62:63], d)
                    m = act(hidn[:, i, :], acc2[o][1][:, 0:62], ACT.Gelu_apprx_tanh, m, bias=pb[:, i:i + 1])
                    banks.free[acc2[o][0]] = compress.done = m

        comp = compress()
        for _ in linear_g(h, w, 4, 8, rope_into(lambda o: q[:, o, :], sq, T, cc("cos"), cc("sin")), first=0):
            next(comp, None)
        for _ in linear_g(h, w, 2, 8, rope_into(lambda o: kk[:, o, :], sq, T, cc("cos"), cc("sin")), first=4):
            next(comp, None)
        linear_tok(h, io["w_cv"], 280, lambda t, a, d: act(vt[:, t, :], a, ACT.Copy, d))
        run(comp)
        gt = alloc(NT * 24).rearrange("p (t c) -> p t c", t=NT)
        act(gt, vt[:, :, 256:280], ACT.Sigmoid)
        m = compress.done
        pe.wait(m, m_w2)
        b, acc = bank()
        for g in range(2):
            for o in range(2):
                d = mm(acc[64 * g:64 * g + 64, 0:31], w2[:, o, :], hidn[:, o, 31 * g:31 * g + 31],
                       o == 0, o == 1, mark=True)
        banks.free[b] = rope_into(lambda o: kcm, sq, 31, cc("ccos"), cc("csin"))(0, acc[:, 0:31], d)
        b, acc = bank()
        for g in range(2):
            for o in range(2):
                d = mm(acc[0:31, 64 * g:64 * g + 64], hidn[:, 2 + o, 31 * g:31 * g + 31], w2[:, 2 + o, :],
                       o == 0, o == 1, mark=True)
        banks.free[b] = act(vcm[0:31, :], acc[0:31, 0:128], ACT.Copy, d)
        pe.wait(dv.last(), ac.last())

        heads = {}

        def unit(hd, t, g):
            if (t, g) == (0, 0):
                heads[hd] = bank()
            ob = heads[hd]
            nk = (t + 1) * P
            r = slice(64 * g, 64 * g + 64)
            qt = q[r, hd, t * P:(t + 1) * P]
            out = ob[1][r, t * P:(t + 1) * P]
            head = 4 * g + hd
            parts = [(kcm[r, :], 31, [(0, 31, cc("cmpmask", 31 * t, 31))]),
                     (kk[r, 0, 0:nk], nk, [(t * P, nk, cc("negmask"))]),
                     (kk[r, 1, 0:nk], nk, [(t * P, nk, cc("negmask"))])]
            prs = [at.probs(qt, keys, n, masks) for keys, n, masks in parts]
            yield
            ready = []
            for br, (i, pr, j, s4, m) in enumerate(prs):
                n = parts[br][1]
                recip(s4[:, 3:4], s4[:, 2:3], m)
                tt(dv, s4[:, 3:4], s4[:, 3:4], gt[:, t, 3 * head + br:3 * head + br + 1], MUL)
                if br == 0:
                    tt(dv, s4[:, 3:4], s4[:, 3:4], cc("cmprow", t, 1), MUL)
                m = ts(dv, pr[:, 0:n], pr[:, 0:n], s4[:, 3:4], None, MUL, None)
                at.st.free[j] = m
                ready.append(m)
            yield
            tp = []
            for br, (i, pr, j, s4, _) in enumerate(prs):
                ip, pt, m, d = at.transpose(pr, parts[br][1], ready[br])
                at.pr.free[i] = d
                tp.append((ip, pt, m))
            yield
            ip, pt, m = tp[0]
            pe.wait(m)
            at.pt.free[ip] = mm(out, vcm[0:31, r], pt[0:31, 0:128], True, False, mark=True)
            for br in (1, 2):
                ip, pt, m = tp[br]
                pe.wait(m)
                for kt in range(t + 1):
                    d = mm(out, vt[:, kt, 128 * (br - 1) + 64 * g:128 * (br - 1) + 64 * g + 64],
                           pt[:, kt * P:(kt + 1) * P], False, br == 2 and kt == t,
                           mark=(kt == t))
                at.pt.free[ip] = d
            if (t, g) == (NT - 1, 1):
                banks.free[ob[0]] = act(y[:, hd, :], ob[1], ACT.Copy, d)

        weave((unit(hd, t, g) for hd in range(4) for t in range(NT) for g in range(2)), 4)
        barrier()

        top[0] = keep
        qk = tiles(4)
        vt = tiles(4)
        raw = alloc(2 * (T + 3)).rearrange("p (k n) -> p k n", k=2)
        s1, s2, s3 = alloc(T), alloc(T), alloc(T)
        og = tiles(4)
        rows = tiles(4)
        cT = alloc(16)
        memset(po, raw[:, :, 0:3], 0.0)

        def conv(o, acc, d):
            r = raw[:, o % 2, :]
            m = act(r[:, 3:T + 3], acc, ACT.Copy, d, dv.last(), po.last())
            ts(dv, s1, r[:, 0:T], pc("mconv_w", 4 * o), pc("mconv_b", o), MUL, ADD, m)
            for k in range(1, 4):
                mc = stt(s1, r[:, k:k + T], pc("mconv_w", 4 * o + k), s1, MUL, ADD)
            act(qk[:, o, :], s1, ACT.Silu, mc)
            dv.wait(ac.last())
            return m

        linear(h, w, 4, 8, conv, first=10)
        for o in range(2):
            ts(dv, qk[:, o, :], qk[:, o, :], 0.125, None, MUL, None)
        linear(h, w, 4, 8, lambda o, a, d: act(og[:, o, :], a, ACT.Sigmoid, d), first=14)
        linear_tok(h, io["w_dv"], T, lambda t, a, d: act(vt[:, t, :], a, ACT.Copy, d))
        fi = {}

        def gates(o, acc, d):
            m = ts(dv, s1[0:36, :], acc[0:36, :], pc("gate_b")[0:36, :], None, ADD, None, d)
            return m

        linear(h, w, 1, 8, gates, first=18)
        R = lambda a: a[32:36, :]
        m = act(R(s2), R(s1), ACT.Abs, dv.last())
        m = act(R(s2), R(s2), ACT.Exp, scale=-1.0)
        m = act(R(s2), R(s2), ACT.Ln, bias=1.0)
        ts(dv, R(s3), R(s1), 0.0, None, MIN, None, m)
        tt(dv, R(s3), R(s3), R(s2), SUB)
        Fr = rows[:, 0, :]
        dv.do(lambda e: e.tensor_tensor_scan(R(Fr), R(cst[:, CC["ones"]:CC["ones"] + 1])
                                             .to_broadcast([4, T]), R(s3), 0.0, MUL, ADD))
        mF = dv.last()
        b, acc = bank()
        pe.wait(mF)
        d = mm(acc[0:4, :], cst[32:36, CC["ident"] + 32:CC["ident"] + 36], Fr[32:36, :], True, True,
               mark=True)
        F0, G0, C0 = rows[0:4, 1, :], rows[0:4, 2, :], rows[0:4, 3, :]
        banks.free[b] = copy(dv, F0, acc[0:4, :], d)
        tt(dv, C0, s1[0:4, :], F0, SUB)
        one = cst[0:4, CC["ones"]:CC["ones"] + 1].to_broadcast([4, T])
        dv.do(lambda e: e.tensor_tensor_scan(G0, one, C0, 0.0, MUL, MAX))
        tt(dv, F0, F0, G0, ADD)
        ts(dv, F0, F0, -1.0, 85.0, MUL, MIN)
        ts(dv, F0, F0, -85.0, None, MAX, None)
        m = ts(dv, G0, G0, -1.0, None, MUL, None)
        b, acc = bank()
        pe.wait(m)
        for t in range(NT):
            d = tr(acc[:, 4 * t:4 * t + 4], C0[:, t * P:(t + 1) * P], mark=True)
        banks.free[b] = copy(dv, cT, acc[:, 0:16], d)
        pe.wait(dv.last(), ac.last())
        es = Ring([alloc(T) for _ in range(4)])
        gm = Ring([(alloc(T), alloc(T)) for _ in range(2)])
        fin = Ring([(s1, s2)])
        heads = {}

        def unit(hd, s):
            r = slice(64 * (hd % 2), 64 * (hd % 2) + 64)
            if s == 0:
                sel = cst[0:4, CC["sel"] + 128 * hd:CC["sel"] + 128 * hd + 128]
                i, (gt_, mt_), f = gm.take()
                bG, aG = bank()
                dG = mm(aG, sel, G0, True, True, mark=True)
                bM, aM = bank()
                dM = mm(aM, sel, F0, True, True, mark=True)
                mG = act(gt_, aG, ACT.Copy, dG, f)
                banks.free[bG] = mG
                mM = act(mt_, aM, ACT.Exp, dM)
                banks.free[bM] = mM
                heads[hd] = (i, gt_, mt_, mG, mM, bank(), bank())
            gi, gt_, mt_, mG, mM, (bn, an), (bd, ad) = heads[hd]
            n0 = s * P
            bs, as_ = bank()
            ds = mm(as_[:, n0:T], qk[r, 2 + hd // 2, n0:n0 + P], qk[r, hd // 2, n0:T], True, True, mark=True)
            j, e1, f = es.take()
            m = ts(dv, e1[:, n0:T], gt_[:, n0:T], cT[:, 4 * s + hd:4 * s + hd + 1], 0.0, ADD, MIN, mG, f)
            m = act(e1[:, n0:T], e1[:, n0:T], ACT.Exp, m)
            yield
            tt(dv, e1[:, n0:n0 + P], e1[:, n0:n0 + P], cc("triu"), MUL, m)
            m = tt(dv, e1[:, n0:T], e1[:, n0:T], as_[:, n0:T], MUL, ds)
            banks.free[bs] = m
            yield
            pe.wait(m)
            mm(an[:, n0:T], vt[:, s, hd * P:(hd + 1) * P], e1[:, n0:T], s == 0, s == 3)
            d = mm(ad[:, n0:T], ones, e1[:, n0:T], s == 0, s == 3, mark=True)
            es.free[j] = d
            if s < NT - 1:
                return
            fi, (a_, b_), f = fin.take()
            m = act(a_, ad, ACT.Abs, d, f)
            banks.free[bd] = m
            yield
            mt2 = tt(dv, a_, a_, mt_, MAX, m, mM)
            gm.free[gi] = mt2
            recip(a_, a_)
            m = tt(dv, a_, a_, an, MUL)
            banks.free[bn] = m
            m = act(b_, a_, ACT.Square, m)
            yield
            b, acc = bank()
            pe.wait(m)
            d = mm(acc, ones, b_, True, True, mark=True)
            m, banks.free[b] = rstd_of(acc, b_, 1.0 / 128, 1e-6, d)
            yield
            stt(a_, a_, pc("mnorm", hd), b_, MUL, MUL, m)
            fin.free[fi] = tt(dv, y[:, 4 + hd, :], a_, og[:, hd, :], MUL)

        weave((unit(hd, s) for hd in range(4) for s in range(NT)), 3)
        pair_up([y[:, k, :] for k in range(8)], h, dv.last(), ac.last(), pe.last())
        linear(h, io["w_cd_out"], 8, 8, residual_to(residual))
        barrier()

    steps = [
        even,
        odd,
        lambda: swiglu("ffa_norm", 0, io["ffa_gate"], io["ffa_up"], io["ffa_down"]),
        mixer_ab,
        lambda: swiglu("ffb_norm", 0, io["ffb_gate"], io["ffb_up"], io["ffb_down"]),
        lambda: swiglu("ffa_norm", 1, io["ffa_gate"], io["ffa_up"], io["ffa_down"]),
        mixer_cd,
        lambda: swiglu("ffb_norm", 1, io["ffb_gate"], io["ffb_up"], io["ffb_down"]),
    ]
    for f in steps:
        f()
    normed(cur[0], lambda k: pc("final_norm_2", k), 1e-6)
    barrier()
    m = dv.last()
    mo = s_out.start(sp, io["out"], x, m)
    sp.wait(mo)

    return pe, dv, ac, po, sp


def _constants():
    f = np.float32
    c = np.zeros((P, NCONST), f)

    def put(name, a):
        a = np.asarray(a, f)
        c[:a.shape[0], CC[name]:CC[name] + a.shape[1]] = a

    i = np.arange(P)
    put("ident", np.eye(P))
    put("ones", np.ones((P, P)))
    put("bones", (i[:, None] // 64 == i[None, :] // 64))
    R = np.zeros((P, P), f)
    for b in (0, 64):
        for d in range(32):
            R[b + d + 32, b + d] = -1
            R[b + d, b + d + 32] = 1
    put("rot", R)
    inv = (10000.0 ** (-np.arange(0, 64, 2, dtype=f) / 64)).astype(f)

    def tabs(pos):
        ang = pos.astype(f)[None, :] * np.tile(inv, 4)[:, None]
        return np.cos(ang), np.sin(ang)

    a, b = tabs(np.arange(T))
    put("cos", a)
    put("sin", b)
    ends = 16 * np.arange(31) + 31
    a, b = tabs(ends)
    put("ccos", a)
    put("csin", b)
    put("negmask", np.where(i[None, :] <= i[:, None], 0.0, NEG))
    t = np.arange(T).reshape(4, P)
    put("cmpmask", np.concatenate([np.where(ends[None, :] <= t[k][:, None], 0.0, NEG) for k in range(4)], 1))
    put("cmprow", (t.T >= 31))
    same = i[:, None] // 32 == i[None, :] // 32
    strict = same & (i[:, None] < i[None, :])
    incl = same & (i[:, None] <= i[None, :])
    put("ml", np.concatenate([strict * 1.0, incl * 1.0, incl * -1.0], 1))
    put("nstrict", strict * -1.0)
    cm = i[:, None] // 32 == np.arange(4)[None, :]
    put("cm", cm)
    put("ncm", cm * -1.0)
    put("scanm", np.tile((np.arange(T) % 32 != 0)[None, :], (P, 1)))
    put("triu", i[:, None] <= i[None, :])
    put("ident64", np.tile(np.eye(64), (2, 1)))
    put("eye32", np.tile(np.eye(32).reshape(1, -1), (P, 1)))
    sel = np.zeros((4, 512), f)
    for k in range(4):
        sel[k, 128 * k:128 * k + 128] = 1
    put("sel", sel)
    pos = np.arange(1, 17, dtype=f)
    put("invpos", np.tile(np.concatenate([1 / np.minimum(pos, f(w)) for w in (2, 4, 8, 16)])[None, :], (P, 1)))
    return c


def _w(a):
    k, m = a.shape
    return np.ascontiguousarray(a.reshape(k // P, P, m // P, P).transpose(2, 1, 0, 3)).reshape(m // P, P, k)


def _col(v):
    return np.ascontiguousarray(v.reshape(-1, P).T)


def _layout(i):
    f = np.float32
    prm = np.zeros((P, NCOL), f)

    def put(name, a):
        prm[:a.shape[0], COL[name]:COL[name] + a.shape[1]] = a

    for name, key in [("even_norm", "even_norm"), ("pool_scale", "pool_scale"), ("ssm_d", "ssm_d"),
                      ("odd_norm", "odd_norm"), ("conv_b", "conv_b"), ("ln_g", "conv_ln_g"),
                      ("ln_b", "conv_ln_b"), ("mu", "rwkv_mu_2"), ("w0", "rwkv_w0_2"), ("a0", "rwkv_a0_2"),
                      ("kk", "rwkv_kk_2"), ("ka", "rwkv_ka_2"), ("lnw", "rwkv_lnw_2"), ("lnb", "rwkv_lnb_2"),
                      ("subln", "diff_subln_2"), ("mconv_b", "mlstm_conv_b_2"), ("mnorm", "mlstm_norm_2")]:
        put(name, _col(i[key][0]))
    put("final_norm", _col(i["final_norm"]))
    put("final_norm_2", _col(i["final_norm_2"]))
    for n in ("ffa_norm", "mix_norm", "ffb_norm"):
        put(n, _col(i[n + "_2"].reshape(-1)))
    put("rk", _col(i["rwkv_rk_2"][0].reshape(-1)))
    put("log_dt", np.repeat(i["ssm_log_dt"][0].reshape(16, 2).T, 64, axis=0))
    put("a_re", i["ssm_a_re"][0].reshape(16, P).T)
    put("a_im", i["ssm_a_im"][0].reshape(16, P).T)
    put("conv_w", i["conv_w"][0].reshape(31, 8, P).transpose(2, 1, 0).reshape(P, 248))
    put("mconv_w", i["mlstm_conv_w_2"][0].reshape(4, 4, P).transpose(2, 1, 0).reshape(P, 16))
    gb = np.zeros((P, 1), f)
    gb[0:4, 0] = i["mlstm_ig_b_2"][0]
    gb[32:36, 0] = i["mlstm_fg_b_2"][0]
    put("gate_b", gb)
    put("lam", np.tile(i["diff_lam_2"][0].reshape(1, 256), (P, 1)))
    put("pe_k", i["nsa_pe_k_2"][0].reshape(16, P).T)
    put("pe_v", i["nsa_pe_v_2"][0].reshape(16, P).T)

    out = {"params": prm, "consts": _constants()}
    out["x"] = np.ascontiguousarray(i["x"][0].T.reshape(8, P, T).transpose(1, 0, 2))
    out["w_even"] = _w(i["even_w_in"][0])
    out["w_glu"] = _w(i["ssm_w_glu"][0])
    out["w_even_out"] = _w(i["even_w_out"][0])
    out["pool_w"] = np.ascontiguousarray(i["pool_w"][0].transpose(1, 0, 2)).reshape(P, 512)
    for n in ("re", "im"):
        b = i["ssm_b_" + n][0].reshape(4, 4, 2, 64, 16)
        z = np.zeros((4, 2, 16, 4, 2, 64), f)
        for g in range(2):
            z[:, g, :, :, g, :] = b[:, :, g].transpose(1, 3, 0, 2)
        out["b_" + n] = z.reshape(P, 512)
    cs = []
    for n in ("re", "im"):
        c = i["ssm_c_" + n][0].reshape(16, 2, 16, 64)
        z = np.zeros((2, 64, 16, 2, 16), f)
        for g in range(2):
            z[g, :, :, g, :] = c[:, g].transpose(2, 0, 1)
        cs.append(z.reshape(P, 512))
    out["c_bd"] = np.concatenate(cs, 1)
    out["w_odd"] = _w(i["odd_w_in"][0])
    out["w_odd_out"] = _w(i["odd_w_out"][0])
    for n in ("ffa", "ffb"):
        for m in ("gate", "up", "down"):
            out[f"{n}_{m}"] = np.stack([_w(a) for a in i[f"{n}_{m}_2"]])
    ab = i["ab_w_in_2"][0]
    out["w_ab"] = _w(np.concatenate([ab[:, :1024], ab[:, 1536:]], 1))
    out["w_av"] = np.ascontiguousarray(ab[:, 1024:1536]).reshape(8, P, 512)
    out["w_ab_out"] = _w(i["ab_w_out_2"][0])
    out["w2a2"] = np.concatenate([i["rwkv_w2_2"][0], i["rwkv_a2_2"][0]], 0)
    out["g2"] = np.ascontiguousarray(i["rwkv_g2_2"][0])
    cd = i["cd_w_in_2"][0]
    qc = cd[:, :512].reshape(1024, 2, 4, 64).transpose(0, 2, 1, 3).reshape(1024, 512)
    kc, vc, ks, vs, kw, vw = [cd[:, 512 + 128 * k:640 + 128 * k] for k in range(6)]
    cg = cd[:, 1280:1304]
    dq, dk, dv_ = cd[:, 1304:1560], cd[:, 1560:1816], cd[:, 1816:2328]
    di, df, dog = cd[:, 2328:2332], cd[:, 2332:2336], cd[:, 2336:2848]
    dup = [np.concatenate([z[:, 64 * g:64 * g + 64]] * 2, 1) for z in (kc, vc) for g in range(2)]
    ifg = np.zeros((1024, P), f)
    ifg[:, 0:4] = di
    ifg[:, 32:36] = df
    out["w_cd"] = _w(np.concatenate([qc, ks, kw] + dup + [dq, dk, dog, ifg], 1))
    out["w_cv"] = np.ascontiguousarray(np.concatenate([vs, vw, cg], 1)).reshape(8, P, 280)
    out["w_dv"] = np.ascontiguousarray(dv_).reshape(8, P, 512)
    w1 = np.stack([i["nsa_w1_k_2"][0], i["nsa_w1_v_2"][0]]).reshape(2, 4, 4, P, 256)
    out["nsa_w1"] = np.ascontiguousarray(w1.transpose(0, 1, 3, 2, 4)).reshape(2, 4, P, 1024)
    w2 = np.stack([i["nsa_w2_k_2"][0], i["nsa_w2_v_2"][0]]).reshape(4, P, 64)
    out["nsa_w2"] = np.ascontiguousarray(w2.transpose(1, 0, 2)).reshape(P, 256)
    wo = i["cd_w_out_2"][0]
    oc = wo[:512].reshape(2, 4, 64, 1024).transpose(1, 0, 2, 3).reshape(512, 1024)
    out["w_cd_out"] = _w(np.concatenate([oc, wo[512:]], 0))
    return {k: np.ascontiguousarray(v) for k, v in out.items()}


def kernel(**inputs):
    import concourse.bacc as _bacc
    from concourse.bass_utils import run_bass_kernel_spmd

    arrays = _layout({k: np.asarray(v) for k, v in inputs.items()})
    nc = _bacc.Bacc("TRN2", target_bir_lowering=False, num_devices=1)
    io = {k: nc.dram_tensor(f"in_{k}", a.shape, F32, kind="ExternalInput").ap() for k, a in arrays.items()}
    io["out"] = nc.dram_tensor("out_0", (P, 8, T), F32, kind="ExternalOutput").ap()
    build(nc, io)
    r = run_bass_kernel_spmd(nc, [{f"in_{k}": a for k, a in arrays.items()}], core_ids=[0])
    y = r.results[0]["out_0"]
    return np.ascontiguousarray(y.transpose(2, 1, 0).reshape(1, T, 1024))
```
